# Optimizing a Trainium2 kernel written in Bass

```python
import math
import jax, jax.numpy as jnp
from jax import lax
import numpy as np

D_MODEL = 2048
BATCH = 1
SEQ = 256
DEPTH = 2
DEC_BATCH = 8
DEC_SEQ = 8
PAST_LEN = 2048
PAGE_SIZE = 128

N_META = 16
N_EVEN = (DEPTH + 1) // 2
N_ODD = DEPTH // 2
D_A = D_MODEL // 2
H_A = 8
BS_A = D_A // H_A
CONV_A = 4
C_RG = 8.0
D_B = D_MODEL // 2
H_B = 8
DK_B = D_B // H_B
DV_B = D_B // H_B
CHUNK_B = 64
LB_FLOOR = 1e-30
D_C = D_MODEL // 2
GROUP_C = 16
G_C = D_C // GROUP_C
P_C = 64
D_FF = ((8 * D_MODEL // 3 + 127) // 128) * 128
CONV_F = 3
EPS = 1e-6
EVEN_SPLITS = (D_A, D_A, D_B, D_B, D_B, D_B)
EVEN_SPLIT_IDX = tuple(int(v) for v in np.cumsum(EVEN_SPLITS)[:-1])

kernel_name = "hybrid_rglru_hgrn2_s5_convffn_step"

F32 = jnp.float32

def rmsnorm(x, g):
    xf = x.astype(F32)
    y = xf * lax.rsqrt(jnp.mean(xf * xf, axis=-1, keepdims=True) + EPS)
    return (y * g.astype(F32)).astype(x.dtype)

def causal_dwconv(x, buf, w, b):
    width = w.shape[0]
    T = x.shape[1]
    xp = jnp.concatenate([buf.astype(x.dtype), x], axis=1)
    y = jnp.zeros_like(x) + b.astype(x.dtype)
    for k in range(width):
        y = y + w[k].astype(x.dtype) * xp[:, k:k + T]
    return y, xp[:, T:]

def linear_scan(a, b):
    def comb(l, r):
        al, bl = l
        ar, br = r
        return al * ar, ar * bl + br
    _, h = lax.associative_scan(comb, (a, b), axis=1)
    return h

def complex_scan(ar, ai, br, bi):
    def comb(l, r):
        a1r, a1i, b1r, b1i = l
        a2r, a2i, b2r, b2i = r
        return (a2r * a1r - a2i * a1i, a2r * a1i + a2i * a1r,
                a2r * b1r - a2i * b1i + b2r, a2r * b1i + a2i * b1r + b2i)
    _, _, sr, si = lax.associative_scan(comb, (ar, ai, br, bi), axis=1)
    return sr, si

def rg_lru(xc, h0, w_r, b_r, w_i, b_i, lam, reset_first):
    B_, T, _ = xc.shape
    xf = xc.astype(F32)
    xh = xf.reshape(B_, T, H_A, BS_A)
    r = jax.nn.sigmoid(jnp.einsum('bthi,hij->bthj', xh, w_r.astype(F32)) + b_r.astype(F32)).reshape(B_, T, D_A)
    ig = jax.nn.sigmoid(jnp.einsum('bthi,hij->bthj', xh, w_i.astype(F32)) + b_i.astype(F32)).reshape(B_, T, D_A)
    log_a = -C_RG * r * jax.nn.softplus(-lam.astype(F32))
    a = jnp.exp(log_a)
    mult = jnp.sqrt(-jnp.expm1(2.0 * log_a))
    if reset_first:
        mult = mult.at[:, 0].set(1.0)
    b = mult * ig * xf
    b = b.at[:, 0].add(a[:, 0] * h0.astype(F32))
    h = linear_scan(a, b)
    return h, h[:, -1]

def gla_chunk(S0, q, logf, k, v):
    C = q.shape[1]
    bcum = jnp.cumsum(logf, axis=1)
    causal = jnp.tril(jnp.ones((C, C), dtype=bool))[None, :, :, None, None]
    diff = bcum[:, :, None] - bcum[:, None, :]
    decay = jnp.where(causal, jnp.exp(jnp.where(causal, diff, 0.0)), 0.0)
    attn = jnp.einsum('bthk,btshk,bshk->bhts', q, decay, k)
    o = jnp.einsum('bhts,bshv->bthv', attn, v) + jnp.einsum('bthk,bhkv->bthv', q * jnp.exp(bcum), S0)
    b_end = bcum[:, -1]
    kd = k * jnp.exp(b_end[:, None] - bcum)
    S = jnp.exp(b_end)[..., None] * S0 + jnp.einsum('bshk,bshv->bhkv', kd, v)
    return S, o

def hgrn2(q, fz, v, g, S0, lb, gn, is_prompt):
    B_, T, _ = q.shape
    qf = q.astype(F32).reshape(B_, T, H_B, DK_B)
    fzf = fz.astype(F32).reshape(B_, T, H_B, DK_B)
    vf = v.astype(F32).reshape(B_, T, H_B, DV_B)
    lbh = jnp.clip(lb.astype(F32), 0.0, 1.0).reshape(H_B, DK_B)
    logf = jnp.logaddexp(jnp.log(jnp.maximum(lbh, LB_FLOOR)), jnp.log1p(-lbh) + jax.nn.log_sigmoid(fzf))
    k = (1.0 - lbh) * jax.nn.sigmoid(-fzf)
    if is_prompt:
        S, o_meta = gla_chunk(S0, qf[:, :N_META], logf[:, :N_META], k[:, :N_META], vf[:, :N_META])
        n = (T - N_META) // CHUNK_B

        def to_chunks(t):
            return t[:, N_META:].reshape(B_, n, CHUNK_B, H_B, t.shape[-1]).swapaxes(0, 1)

        def step(S_c, inp):
            return gla_chunk(S_c, *inp)

        S, o_c = lax.scan(step, S, (to_chunks(qf), to_chunks(logf), to_chunks(k), to_chunks(vf)))
        o_real = o_c.swapaxes(0, 1).reshape(B_, T - N_META, H_B, DV_B)
        o = jnp.concatenate([o_meta, o_real], axis=1)
    else:
        S, o = gla_chunk(S0, qf, logf, k, vf)
    o = o * lax.rsqrt(jnp.mean(o * o, axis=-1, keepdims=True) + EPS)
    o = o.reshape(B_, T, D_B) * gn.astype(F32) * jax.nn.silu(g.astype(F32))
    return o, S

def s5(u, s0_re, s0_im, lam_re, lam_im, log_dt, bmat_re, bmat_im, cmat_re, cmat_im, d_skip):
    B_, T, _ = u.shape
    uf = u.astype(F32).reshape(B_, T, G_C, GROUP_C)
    lr = lam_re.astype(F32)
    li = lam_im.astype(F32)
    dt = jnp.exp(log_dt.astype(F32))[:, None]
    mag = jnp.exp(lr * dt)
    ar = mag * jnp.cos(li * dt)
    ai = mag * jnp.sin(li * dt)
    den = lr * lr + li * li
    zr = ((ar - 1.0) * lr + ai * li) / den
    zi = (ai * lr - (ar - 1.0) * li) / den
    br_ = bmat_re.astype(F32)
    bi_ = bmat_im.astype(F32)
    bb_re = zr[..., None] * br_ - zi[..., None] * bi_
    bb_im = zr[..., None] * bi_ + zi[..., None] * br_
    xr = jnp.einsum('btgc,gpc->btgp', uf, bb_re)
    xi = jnp.einsum('btgc,gpc->btgp', uf, bb_im)
    s0r = s0_re.astype(F32)
    s0i = s0_im.astype(F32)
    xr = xr.at[:, 0].add(ar * s0r - ai * s0i)
    xi = xi.at[:, 0].add(ar * s0i + ai * s0r)
    sr, si = complex_scan(jnp.broadcast_to(ar, xr.shape), jnp.broadcast_to(ai, xr.shape), xr, xi)
    y = (jnp.einsum('btgp,gcp->btgc', sr, cmat_re.astype(F32))
         - jnp.einsum('btgp,gcp->btgc', si, cmat_im.astype(F32))
         + d_skip.astype(F32).reshape(G_C, GROUP_C) * uf)
    return y.reshape(B_, T, D_C), sr[:, -1], si[:, -1]

def conv_ffn(x, buf, g, w_up, w_gate, cw, cb, w_down):
    h = rmsnorm(x, g)
    up = h @ w_up.astype(x.dtype)
    upc, new_buf = causal_dwconv(up, buf, cw, cb)
    act = jax.nn.gelu(upc) * (h @ w_gate.astype(x.dtype))
    return x + act @ w_down.astype(x.dtype), new_buf

def trunk(x, a_conv, a_h, b_S, c_re, c_im, f_conv, is_prompt,
          g_mix, w_in_e, conv_a_w, conv_a_b, w_ra, b_ra, w_ia, b_ia, lam_a, lb_all, gn_b, w_out_e,
          w_in_c, lam_re, lam_im, log_dt, bmat_re, bmat_im, cmat_re, cmat_im, d_skip, w_glu_v, w_glu_g,
          g_ffn, w_up, w_gate, conv_f_w, conv_f_b, w_down, g_final):
    n_a_conv, n_a_h, n_b_S, n_c_re, n_c_im, n_f = [], [], [], [], [], []
    dt_ = x.dtype
    for l in range(DEPTH):
        h = rmsnorm(x, g_mix[l])
        if l % 2 == 0:
            i = l // 2
            z = h @ w_in_e[i].astype(dt_)
            xa, ga, q, fz, v, gb = jnp.split(z, EVEN_SPLIT_IDX, axis=-1)
            xc, nb = causal_dwconv(xa, a_conv[i], conv_a_w[i], conv_a_b[i])
            ha, hl = rg_lru(xc, a_h[i], w_ra[i], b_ra[i], w_ia[i], b_ia[i], lam_a[i], is_prompt)
            out_a = ha * jax.nn.gelu(ga.astype(F32))
            out_b, S = hgrn2(q, fz, v, gb, b_S[i].astype(F32), lb_all[i], gn_b[i], is_prompt)
            mix = jnp.concatenate([out_a, out_b], axis=-1).astype(dt_) @ w_out_e[i].astype(dt_)
            n_a_conv.append(nb)
            n_a_h.append(hl)
            n_b_S.append(S)
        else:
            j = l // 2
            u = h @ w_in_c[j].astype(dt_)
            y, sr, si = s5(u, c_re[j], c_im[j], lam_re[j], lam_im[j], log_dt[j],
                           bmat_re[j], bmat_im[j], cmat_re[j], cmat_im[j], d_skip[j])
            y = jax.nn.gelu(y).astype(dt_)
            mix = (y @ w_glu_v[j].astype(dt_)) * jax.nn.sigmoid(y @ w_glu_g[j].astype(dt_))
            n_c_re.append(sr)
            n_c_im.append(si)
        x = x + mix
        x, fb = conv_ffn(x, f_conv[l], g_ffn[l], w_up[l], w_gate[l], conv_f_w[l], conv_f_b[l], w_down[l])
        n_f.append(fb)
    y = rmsnorm(x, g_final)
    return (y, jnp.stack(n_a_conv), jnp.stack(n_a_h), jnp.stack(n_b_S),
            jnp.stack(n_c_re), jnp.stack(n_c_im), jnp.stack(n_f))

def setup_inputs(seed: int = 0) -> dict:
    key = jax.random.key(seed)
    ks = iter(jax.random.split(key, 64))

    def nrm(shape, scale):
        return scale * jax.random.normal(next(ks), shape, F32)

    u_a = jax.random.uniform(next(ks), (N_EVEN, D_A), F32, 0.9, 0.999)
    a_base = u_a ** (1.0 / C_RG)
    lam_a = jnp.log(a_base) - jnp.log1p(-a_base)
    lam_im = math.pi * jnp.arange(P_C, dtype=F32)[None, None, :] + nrm((N_ODD, G_C, P_C), 0.01)
    log_dt = jax.random.uniform(next(ks), (N_ODD, G_C), F32, math.log(0.001), math.log(0.1))
    return {
        "x_prompt": nrm((BATCH, SEQ, D_MODEL), 1.0),
        "x_sample": nrm((DEC_BATCH, DEC_SEQ, D_MODEL), 1.0),
        "state_a_conv": nrm((N_EVEN, DEC_BATCH, CONV_A - 1, D_A), 1.0),
        "state_a_h": nrm((N_EVEN, DEC_BATCH, D_A), 0.5),
        "state_b_S": nrm((N_EVEN, DEC_BATCH, H_B, DK_B, DV_B), 0.5),
        "state_c_re": nrm((N_ODD, DEC_BATCH, G_C, P_C), 0.3),
        "state_c_im": nrm((N_ODD, DEC_BATCH, G_C, P_C), 0.3),
        "state_ffn_conv": nrm((DEPTH, DEC_BATCH, CONV_F - 1, D_FF), 1.0),
        "meta_tokens": nrm((N_META, D_MODEL), 1.0),
        "g_mix": 1.0 + nrm((DEPTH, D_MODEL), 0.05),
        "w_in_e": nrm((N_EVEN, D_MODEL, sum(EVEN_SPLITS)), D_MODEL ** -0.5),
        "conv_a_w": nrm((N_EVEN, CONV_A, D_A), CONV_A ** -0.5),
        "conv_a_b": nrm((N_EVEN, D_A), 0.01),
        "w_ra": nrm((N_EVEN, H_A, BS_A, BS_A), BS_A ** -0.5),
        "b_ra": nrm((N_EVEN, H_A, BS_A), 0.01),
        "w_ia": nrm((N_EVEN, H_A, BS_A, BS_A), BS_A ** -0.5),
        "b_ia": nrm((N_EVEN, H_A, BS_A), 0.01),
        "lam_a": lam_a,
        "lb_logits": nrm((N_EVEN, D_B), 1.0),
        "gn_b": 1.0 + nrm((N_EVEN, D_B), 0.05),
        "w_out_e": nrm((N_EVEN, D_A + D_B, D_MODEL), (D_A + D_B) ** -0.5),
        "w_in_c": nrm((N_ODD, D_MODEL, D_C), D_MODEL ** -0.5),
        "lam_re": -0.5 + nrm((N_ODD, G_C, P_C), 0.01),
        "lam_im": lam_im,
        "log_dt": log_dt,
        "bmat_re": nrm((N_ODD, G_C, P_C, GROUP_C), (2 * GROUP_C) ** -0.5),
        "bmat_im": nrm((N_ODD, G_C, P_C, GROUP_C), (2 * GROUP_C) ** -0.5),
        "cmat_re": nrm((N_ODD, G_C, GROUP_C, P_C), P_C ** -0.5),
        "cmat_im": nrm((N_ODD, G_C, GROUP_C, P_C), P_C ** -0.5),
        "d_skip": nrm((N_ODD, D_C), 0.5),
        "w_glu_v": nrm((N_ODD, D_C, D_MODEL), D_C ** -0.5),
        "w_glu_g": nrm((N_ODD, D_C, D_MODEL), D_C ** -0.5),
        "g_ffn": 1.0 + nrm((DEPTH, D_MODEL), 0.05),
        "w_up": nrm((DEPTH, D_MODEL, D_FF), D_MODEL ** -0.5),
        "w_gate": nrm((DEPTH, D_MODEL, D_FF), D_MODEL ** -0.5),
        "conv_f_w": nrm((DEPTH, CONV_F, D_FF), CONV_F ** -0.5),
        "conv_f_b": nrm((DEPTH, D_FF), 0.01),
        "w_down": nrm((DEPTH, D_FF, D_MODEL), D_FF ** -0.5),
        "g_final": 1.0 + nrm((D_MODEL,), 0.05),
    }

def reference(x_prompt, x_sample, state_a_conv, state_a_h, state_b_S, state_c_re, state_c_im, state_ffn_conv,
              meta_tokens, g_mix, w_in_e, conv_a_w, conv_a_b, w_ra, b_ra, w_ia, b_ia, lam_a, lb_logits, gn_b,
              w_out_e, w_in_c, lam_re, lam_im, log_dt, bmat_re, bmat_im, cmat_re, cmat_im, d_skip,
              w_glu_v, w_glu_g, g_ffn, w_up, w_gate, conv_f_w, conv_f_b, w_down, g_final):
    sm = jax.nn.softmax(lb_logits.astype(F32), axis=0)
    lb_all = jnp.clip(jnp.cumsum(sm, axis=0) - sm[0:1], 0.0, 1.0)
    B_ = x_prompt.shape[0]
    dtp = x_prompt.dtype
    meta = jnp.broadcast_to(meta_tokens.astype(dtp)[None], (B_, N_META, D_MODEL))
    xp = jnp.concatenate([meta, x_prompt], axis=1)
    z_a_conv = jnp.zeros((N_EVEN, B_, CONV_A - 1, D_A), dtp)
    z_a_h = jnp.zeros((N_EVEN, B_, D_A), F32)
    z_b_S = jnp.zeros((N_EVEN, B_, H_B, DK_B, DV_B), F32)
    z_c = jnp.zeros((N_ODD, B_, G_C, P_C), F32)
    z_f = jnp.zeros((DEPTH, B_, CONV_F - 1, D_FF), dtp)
    yp, p_a_conv, p_a_h, p_b_S, p_c_re, p_c_im, p_f_conv = trunk(
        xp, z_a_conv, z_a_h, z_b_S, z_c, z_c, z_f, True,
        g_mix, w_in_e, conv_a_w, conv_a_b, w_ra, b_ra, w_ia, b_ia, lam_a, lb_all, gn_b, w_out_e,
        w_in_c, lam_re, lam_im, log_dt, bmat_re, bmat_im, cmat_re, cmat_im, d_skip, w_glu_v, w_glu_g,
        g_ffn, w_up, w_gate, conv_f_w, conv_f_b, w_down, g_final)
    y_prompt = yp[:, N_META:]
    y_sample, s_a_conv, s_a_h, s_b_S, s_c_re, s_c_im, s_f_conv = trunk(
        x_sample, state_a_conv, state_a_h, state_b_S, state_c_re, state_c_im, state_ffn_conv, False,
        g_mix, w_in_e, conv_a_w, conv_a_b, w_ra, b_ra, w_ia, b_ia, lam_a, lb_all, gn_b, w_out_e,
        w_in_c, lam_re, lam_im, log_dt, bmat_re, bmat_im, cmat_re, cmat_im, d_skip, w_glu_v, w_glu_g,
        g_ffn, w_up, w_gate, conv_f_w, conv_f_b, w_down, g_final)
    return (y_prompt, y_sample,
            p_a_conv, p_a_h, p_b_S, p_c_re, p_c_im, p_f_conv,
            s_a_conv, s_a_h, s_b_S, s_c_re, s_c_im, s_f_conv)


_drawn_inputs = setup_inputs


def setup_inputs(seed=0):
    import zlib

    import numpy as np

    out = dict(_drawn_inputs(seed))
    spreads = {}
    factors = {'b_ra': 25.39, 'b_ia': 8.0, 'lam_re': 16.402, 'conv_f_b': 7.998}
    for name, (base, spread) in spreads.items():
        noise = np.random.default_rng([zlib.crc32(name.encode()), seed]).standard_normal(out[name].shape)
        drawn = base * np.exp(spread * noise) if base else spread * noise
        out[name] = __import__('jax').numpy.asarray(drawn.astype(out[name].dtype))
    for name, factor in factors.items():
        out[name] = (out[name] * factor).astype(out[name].dtype)
    return out
```

```python
import numpy as np
import concourse.bass as bass
from concourse import mybir
from contextlib import ExitStack

F32 = mybir.dt.float32
F32R = mybir.dt.float32r
ALU = mybir.AluOpType
ACT = mybir.ActivationFunctionType
ds = bass.ds

P = 128
D = 2048
DC = D // P
META, SEQ = 16, 256
TP = META + SEQ
NS, LS = 8, 8
T = TP + NS * LS
DA = D // 2
HEADS = DA // P
FFC = 43
DFF = FFC * P
EPS = 1e-6
C_RG = 8.0
RING = 4
TILE_K = 8
TW = TILE_K * P
PARTS = [(0, 15), (15, 14), (29, 14)]
G5, C5, P5 = 64, 16, 64
PAIRS = G5 // 2
CH = 16
NCH = T // CH
PCH = TP // CH
UNITS = PCH + NS
POOL_HEAD, DVE_HEAD, ROW_TURNS = 16, 33, 6
CREDIT = 4
BANK_CREDIT = 3

COL = {}
_n = 0
for _name, _w in (("g_mix", 32), ("g_ffn", 32), ("g_final", 16),
                  ("conv_f_w", 258), ("conv_f_b", 86),
                  ("conv_a_w", 32), ("conv_a_b", 8), ("b_ra", 8), ("b_ia", 8), ("lam_a", 8), ("lb", 8),
                  ("gn_b", 8), ("d_skip", 8), ("a_h", 64), ("a_conv", 192)):
    COL[_name] = _n
    _n += _w
PCOLS = _n


class Steps:

    def __init__(self, eng, sem):
        self.eng, self.sem, self.base, self.k, self.i, self.per = eng, sem, 0, 0, None, 0

    def then(self, ins):
        ins.then_inc(self.sem, 1)
        self.k += 1
        if self.i is None:
            self.eng.wait_ge(self.sem, self.base + self.k)
        else:
            self.eng.wait_ge(self.sem, self.i * self.per + (self.base + self.k))

    def enter(self, i, per):
        self.base += self.k
        self.k, self.i, self.per = 0, i, per

    def leave(self, turns):
        assert self.k == self.per, (self.k, self.per)
        self.base += turns * self.per
        self.k, self.i = 0, None


class Phase:
    def __init__(self, name, bodies, tiles, groups, banks, tile0, group0):
        self.name, self.bodies, self.tiles, self.groups, self.banks = name, bodies, tiles, groups, banks
        self.tile0, self.group0 = tile0, group0

    def tile(self, i, j):
        return i * self.tiles + (self.tile0 + j)

    def slot_use(self, i, j):
        return i * (self.tiles // RING) + ((self.tile0 + j) // RING + 1)

    def group(self, i, r):
        return i * self.groups + (self.group0 + r)

    def bank(self, r):
        return r % self.banks


def plan():
    out, t, g = {}, 0, 0
    rows = [("head", HEADS, 12, 6, 3), ("wout", 8, 4, 2, 2)]
    ffn = lambda l: [x for p, (_, n) in enumerate(PARTS)
                     for x in ((f"up{l}{p}", n, 4, 2, 2), (f"down{l}{p}", 8, 4, 2, 2))]
    rows += ffn(0) + [("win", 4, 4, 2, 2), ("glu", 8, 4, 4, 4)] + ffn(1)
    for name, b, ti, gr, banks in rows:
        out[name] = Phase(name, b, ti, gr, banks, t, g)
        t += b * ti
        g += b * gr
    return out, t


def halves(n):
    return [(0, (n + 1) // 2), ((n + 1) // 2, n // 2)]


def conv_row_parts(total, own):
    out = []
    for q in range(-(-total // P)):
        a, b = q * P, min(total, (q + 1) * P)
        if a < own:
            out.append((q, 0, min(b, own) - a, "p", a))
        if b > own:
            lo = max(a, own)
            out.append((q, lo - a, b - lo, "s", lo - own))
    return out


STORES_A = len(conv_row_parts(216, 24)) + 2
STORES_F = len(conv_row_parts(774, 86))
STORES_C = 4


def build(nc, a, o):
    PH, _ = plan()
    ctx = ExitStack()
    with ctx:
        def sb(name, shape, dt=F32):
            return ctx.enter_context(nc.sbuf_tensor(name, shape, dt))

        def sem(name):
            return ctx.enter_context(nc.semaphore(name))

        X = sb("X", [P, DC, T])
        raw = sb("raw", [P, RING, TW])
        wh = sb("wh", [P, RING, TW], F32R)
        wl = sb("wl", [P, RING, TW], F32R)
        prm = sb("prm", [P, PCOLS])
        ident = sb("ident", [P, P])
        ones = sb("ones", [P, P])
        masks = sb("masks", [P, 4])
        rs = sb("rs", [P, T])
        ssq = sb("ssq", [P, T])
        sq = sb("sq", [P, T])
        hlast = sb("hlast", [P, 1 + NS, HEADS])
        ncva = sb("ncva", [P, 1 + NS, 3, HEADS])
        tiny = sb("tiny", [P, 12, HEADS])
        rate, lbm, oml = tiny[:, 0, :], tiny[:, 1, :], tiny[:, 2, :]
        arena = nc.sbuf_base
        arena += -arena % 32

        def place(name, shape, at, dt=F32):
            t = nc.alloc_sbuf_tensor_at(name, shape, dt, offset=arena + at)
            size = 4 * int(np.prod(shape[1:]))
            assert arena + at + size <= nc.sbuf_usable_end, (name, arena + at + size - nc.sbuf_usable_end)
            return t, at + size + (-size % 32)

        act, at_h = place("act", [P, 16, 2, T], 0, F32R)
        h, at_u = place("h", [P, DC, 2, T], at_h, F32R)

        def union(at, *items):
            out = []
            for name, shape in items:
                t, at = place(name, shape, at)
                out.append(t)
            return out

        xin, rows = union(at_u, ("xin", [P, 3, D]), ("rows", [P, 9, P]))
        (XA, CT, IG, AA, HH, GA, Q, FZ, V, GB, SB, K, FM, D1, EN, QF, PB, W, OB, KM, KM3, TK, TV, WR, SS, SR, FE) = union(
            at_u, ("XA", [P, 363]), ("CT", [P, 363]), ("IG", [P, T]), ("AA", [P, T]), ("HH", [P, T]), ("GA", [P, T]),
            ("Q", [P, T]), ("FZ", [P, T]), ("V", [P, T]), ("GB", [P, T]), ("SB", [P, T]), ("K", [P, T]),
            ("FM", [P, T + 1]), ("D1", [P, T]), ("EN", [P, T]), ("QF", [P, T]), ("PB", [P, 2, T]), ("W", [P, T]),
            ("OB", [P, T]), ("KM", [P, 2, 256]), ("KM3", [P, 4, 96]), ("TK", [P, 8, P]), ("TV", [P, 3, P]),
            ("WR", [P, 2, P]), ("SS", [P, NS, P]), ("SR", [P, 8, P]), ("FE", [P, UNITS]))
        slot_bytes = 2 * T * 4
        XC, RT = union(14 * slot_bytes, ("XC", [P, T]), ("RT", [P, T]))
        GG, = union(15 * slot_bytes, ("GG", [P, 2, T]))
        UPW = 2 + TP + NS * (2 + LS)
        UP, CV, GT, AC, SF, NCF, srow, orow = union(
            at_u, ("UP", [P, UPW]), ("CV", [P, UPW]), ("GT", [P, T]), ("AC", [P, T]),
            ("SF", [P, NS * 2, FFC]), ("NCF", [P, 1 + NS, 2, FFC]), ("srow", [P, 6, P]), ("orow", [P, 7, P]))
        xs, _ = place("xs", [P, 2, PAIRS, T], 0)
        U5, CTm, BTm, A5, st5, ys5, tmp5, io5o = union(
            at_u, ("U5", [P, 8, T]), ("CTm", [P, 8, 2, P]), ("BTm", [P, 8, 2, P]), ("A5", [P, 2, 2, PAIRS]),
            ("st5", [P, NS, 2, PAIRS]), ("ys5", [P, 2, T]), ("tmp5", [P, 2, 2 * PAIRS * NS]), ("io5o", [2 * PAIRS, 9, P]))
        r5, CN, CX, Bn, BX, B2, io5, zz = union(
            0, ("r5", [PAIRS, 16, P]), ("CN", [P, 2, 8, P5]), ("CX", [P, 2, 8, P]), ("Bn", [P, 2, PAIRS, C5]),
            ("BX", [P, 2, 8, P]), ("B2", [P, 2, PAIRS, C5]), ("io5", [2 * PAIRS, NS, P]), ("zz", [P, 4, PAIRS]))
        GS, VT = union(at_u, ("GS", [P, T]), ("VT", [P, T]))
        yg, yo = union(at_u, ("yg", [P, 2, T]), ("yo", [P, 3, D]))

        bank = [ctx.enter_context(nc.psum_tensor(f"bank{i}", [P, 512], F32)) for i in range(8)]
        BA = (bank[3], bank[4])
        BM = (bank[5], bank[6])
        BO = bank[7]

        landed = [sem(f"landed{s}") for s in range(RING)]
        rounded = sem("rounded")
        split = sem("split")
        used = sem("used")
        evac = sem("evac")
        h_hi, h_lo = sem("h_hi"), sem("h_lo")
        act_hi, act_lo = sem("act_hi"), sem("act_lo")
        ssq_added = sem("ssq_added")
        ms_done = sem("ms_done")
        ms_inv = sem("ms_inv")
        rstd = sem("rstd")
        dchain, pchain = sem("dchain"), sem("pchain")
        consts_in, rows_in, x_in = sem("consts_in"), sem("rows_in"), sem("x_in")
        rows_t, rows_c = sem("rows_t"), sem("rows_c")
        x_t, x_c = sem("x_t"), sem("x_c")
        once = sem("once")
        lam_v, lam_a = sem("lam_v"), sem("lam_a")
        out_dma = sem("out_dma")
        sg, sk, bandin, sfx, km = sem("sg"), sem("sk"), sem("bandin"), sem("sfx"), sem("km")
        p_ready, a_ready, a_used = sem("p_ready"), sem("a_ready"), sem("a_used")
        conv_in, ct, xc, gates, gates_read = sem("conv_in"), sem("ct"), sem("xc"), sem("gates"), sem("gates_read")
        aa, th, t_in, mu, b_ready, ga, oa = sem("aa"), sem("th"), sem("t_in"), sem("mu"), sem("b_ready"), sem("ga"), sem("oa")
        kt, tk_copied = sem("kt"), sem("tk_copied")
        row_turn = sem("row_turn")
        u_ready, s_done, inter = sem("u_ready"), sem("s_done"), sem("inter")
        sbg, oo, oms, oinv, osq, ob = sem("sbg"), sem("oo"), sem("oms"), sem("oinv"), sem("osq"), sem("ob")
        wr_in, ss_in, s_out = sem("wr_in"), sem("ss_in"), sem("s_out")
        up_in, cv0, cv2, gelu, prod = sem("up_in"), sem("cv0"), sem("cv2"), sem("gelu"), sem("prod")
        sf_in, sf_t, sf_c = sem("sf_in"), sem("sf_t"), sem("sf_c")
        nc_t, nc_c, nc_v = sem("nc_t"), sem("nc_c"), sem("nc_v")
        in5, a5v, a5a, t5, c5, x5, x5a, x5v = (sem(n) for n in ("in5", "a5v", "a5a", "t5", "c5", "x5", "x5a", "x5v"))
        scan5, fs_t, fs_c, y5, y5v, y5g = (sem(n) for n in ("scan5", "fs_t", "fs_c", "y5", "y5v", "y5g"))
        gsig = sem("gsig")
        yg_done, y_t, y_c = sem("yg_done"), sem("y_t"), sem("y_c")

        block = ctx.enter_context(nc.Block())

        def one(t, c):
            return t[:, ds(c, 1), :].rearrange("p a t -> p (a t)")

        def part(t, c, r):
            return t[:, ds(c, 1), r, :].rearrange("p a t -> p (a t)")

        def col(name, k=0):
            return prm[:, COL[name] + k:COL[name] + k + 1]

        def dcol(name, i, k=0):
            return prm[:, ds(i + (COL[name] + k), 1)]

        def padded(t, start, pitch):
            return t[:, start:start + NS * pitch].rearrange("p (s w) -> p s w", w=pitch)

        def samples(t):
            return t[:, TP:T].rearrange("p (s w) -> p s w", w=LS)

        def bands(t, d):
            return t[:, 0:T].rearrange("p (c w) -> p c w", w=CH)[:, :, d:CH]

        XAs, CTs = padded(XA, 3 + TP, 3 + LS), padded(CT, 3 + TP, 3 + LS)
        UPs, CVs = padded(UP, 2 + TP, 2 + LS), padded(CV, 2 + TP, 2 + LS)
        NORMS = {"head": 0, "up00": 1, "win": 2, "up10": 3, "final": 4}

        @block.sync
        def _(e):
            flat = lambda x: x.rearrange("(c p) -> c p", p=P)
            rowsets = [
                [(a["g_mix"].rearrange("l (c p) -> (l c) p", p=P), 32), (a["g_ffn"].rearrange("l (c p) -> (l c) p", p=P), 32),
                 (flat(a["g_final"]), 16)],
                *[[(a["conv_f_w"].rearrange("l k (c p) -> (l k c) p", p=P)[86 * q:86 * q + 86], 86)] for q in range(3)],
                [(a["conv_f_b"].rearrange("l (c p) -> (l c) p", p=P), 86)],
                [(a["conv_a_w"][0].rearrange("k (c p) -> (k c) p", p=P), 32), (flat(a["conv_a_b"][0]), 8),
                 (a["b_ra"][0], 8), (a["b_ia"][0], 8), (flat(a["lam_a"][0]), 8), (flat(a["lb_logits"][0]), 8),
                 (flat(a["gn_b"][0]), 8), (flat(a["d_skip"][0]), 8)],
                [(a["state_a_h"][0].rearrange("s (c p) -> (s c) p", p=P), 64)],
                *[[(a["state_a_conv"][0].rearrange("s r (c p) -> (s r c) p", p=P)[96 * q:96 * q + 96], 96)] for q in range(2)],
            ]
            e.dma_start(ident[:], a["c_ident"]).then_inc(consts_in, 16)
            e.dma_start(masks[:], a["c_masks"]).then_inc(consts_in, 16)
            xp, xsm = a["x_prompt"][0], a["x_sample"].rearrange("s t d -> (s t) d")
            for dst, src in ((xin[0:META, 0, :], a["meta_tokens"]), (xin[META:P, 0, :], xp[0:P - META]),
                             (xin[:, 1, :], xp[P - META:2 * P - META]), (xin[0:META, 2, :], xp[2 * P - META:SEQ]),
                             (xin[META:META + NS * LS, 2, :], xsm)):
                e.dma_start(dst, src).then_inc(x_in, 16)
            for q, sets in enumerate(rowsets):
                r = 0
                for src, n in sets:
                    e.dma_start(rows[r:r + n, q, :], src).then_inc(rows_in, 16)
                    r += n

            def load(ph, i, j, w, k0, kn, c):
                e.wait_ge(split, ph.tile(i, j) + 1)
                e.dma_start(raw[:, j % RING, 0:kn * P].rearrange("p (k n) -> p k n", k=kn),
                            w[k0 * P:(k0 + kn) * P, ds(c, P)].rearrange("(k p) n -> p k n", p=P)) \
                    .then_inc(landed[j % RING], 16)

            ph = PH["head"]
            columns = [2 * DA, 3 * DA, 4 * DA, 0, 5 * DA, DA]
            with e.Fori(0, HEADS) as i:
                for j in range(12):
                    load(ph, i, j, a["w_in_e"][0], 8 * (j % 2), 8, (i + 1) * P + (columns[j // 2] - P))
            with e.Fori(0, 8) as i:
                for j in range(4):
                    load(PH["wout"], i, j, a["w_out_e"][0], 8 * (j % 2), 8, i * (2 * P) + (j // 2) * P)

            def ffn(l):
                for p, (f0, n) in enumerate(PARTS):
                    with e.Fori(0, n) as i:
                        for j in range(4):
                            load(PH[f"up{l}{p}"], i, j, a["w_up" if j < 2 else "w_gate"][l], 8 * (j % 2), 8, i * P + f0 * P)
                    with e.Fori(0, 8) as i:
                        for j in range(4):
                            k0, kn = halves(n)[j % 2]
                            load(PH[f"down{l}{p}"], i, j, a["w_down"][l], f0 + k0, kn, i * (2 * P) + (j // 2) * P)

            ffn(0)
            with e.Fori(0, 4) as i:
                for j in range(4):
                    load(PH["win"], i, j, a["w_in_c"][0], 8 * (j % 2), 8, i * (2 * P) + (j // 2) * P)
            with e.Fori(0, 8) as i:
                for j in range(4):
                    load(PH["glu"], i, j, a["w_glu_v" if j % 2 == 0 else "w_glu_g"][0], 0, 8, i * (2 * P) + (j // 2) * P)
            ffn(1)

        @block.scalar
        def _(e):
            sc = nc.scalar

            def round_tile(ph, i, j):
                e.wait_ge(landed[j % RING], (ph.slot_use(i, j) + 1) * 16)
                e.wait_ge(used, ph.tile(i, j) + 1 + RING)
                sc.activation(wh[:, j % RING, :], raw[:, j % RING, :], ACT.Copy).then_inc(rounded, 1)

            def hi_of_x(ph, i, r, g, c):
                e.wait_ge(evac, ph.group(i, r) + 1 + BANK_CREDIT)
                sc.activation(part(h, c, 0), one(X, c), ACT.Copy, scale=prm[:, ds(c + g, 1)]).then_inc(h_hi, 1)

            def norm_root(n):
                e.wait_ge(ms_inv, n + 1)
                sc.activation(rs[:], rs[:], ACT.Sqrt).then_inc(rstd, 1)

            for q in range(9):
                w = (80, 86, 86, 86, 86, 88, 64, 96, 96)[q]
                c0 = (0, 80, 166, 252, 338, 424, 512, 576, 672)[q]
                e.wait_ge(rows_t, q + 1)
                sc.activation(prm[:, c0:c0 + w], BM[q % 2][:, 0:w], ACT.Copy).then_inc(rows_c, 1)
            e.wait_ge(rows_c, 9)
            for c in range(DC):
                e.wait_ge(x_c, c + 1)
                sc.activation(h[:, c, 0, :], X[:, c, :], ACT.Copy, scale=col("g_mix", c)).then_inc(h_hi, 1)
            e.wait_ge(lam_v, 1)
            sc.activation(tiny[:, 4, :], tiny[:, 3, :], ACT.Exp, scale=-1.0)
            sc.activation(tiny[:, 6, :], tiny[:, 5, :], ACT.Exp).then_inc(lam_a, 1)
            for j in range(RING):
                e.wait_ge(landed[j], 16)
                e.wait_ge(used, j + 1)
                sc.activation(wh[:, j, :], raw[:, j, :], ACT.Copy).then_inc(rounded, 1)
            norm_root(0)

            ph = PH["head"]
            with e.Fori(0, HEADS) as i:
                n = i + 1
                for j in range(12):
                    round_tile(ph, i, j)
                    if j == 3:
                        e.wait_ge(evac, ph.group(i, 1) + 1 + BANK_CREDIT)
                        sc.activation(FM[:, 0:T], FZ[:], ACT.Sigmoid).then_inc(sg, 1)
                        sc.activation(K[:], FZ[:], ACT.Sigmoid, scale=-1.0).then_inc(sk, 1)
                    if j == 7:
                        e.wait_ge(conv_in, n)
                        sc.activation(CT[:, 0:360], XA[:, 3:363], ACT.Identity, scale=dcol("conv_a_w", i, 24),
                                      bias=dcol("conv_a_b", i)).then_inc(ct, 1)
                    if j == 9:
                        e.wait_ge(kt, i * 3 + 1)
                        sc.activation(TK[:, 0:4, :], BM[0][:].rearrange("p (a n) -> p a n", a=4), ACT.Copy).then_inc(tk_copied, 1)
                        e.wait_ge(kt, i * 3 + 2)
                        sc.activation(TK[0:80, 4:8, :], BM[1][0:80, :].rearrange("p (a n) -> p a n", a=4), ACT.Copy) \
                            .then_inc(tk_copied, 1)
                        e.wait_ge(kt, i * 3 + 3)
                        sc.activation(TV[:, 0:2, :], BO[:, 0:256].rearrange("p (a n) -> p a n", a=2), ACT.Copy)
                        sc.activation(TV[0:80, 2, :], BO[0:80, 256:384], ACT.Copy).then_inc(tk_copied, 1)
                        e.wait_ge(evac, ph.group(i, 4) + 1 + BANK_CREDIT)
                        sc.activation(SB[:], GB[:], ACT.Sigmoid).then_inc(sbg, 1)
                    if j == 10:
                        e.wait_ge(gates, n)
                        sc.activation(RT[:], BM[0][:, 0:T], ACT.Sigmoid, bias=dcol("b_ra", i))
                        sc.activation(IG[:], BM[1][:, 0:T], ACT.Sigmoid, bias=dcol("b_ia", i)).then_inc(gates_read, 1)
                        e.wait_ge(gates_read, n)
                        sc.activation(AA[:], RT[:], ACT.Exp, scale=tiny[:, 0, ds(i, 1)]).then_inc(aa, 1)
                        sc.activation(CT[:, 0:T], RT[:], ACT.Tanh, scale=tiny[:, 0, ds(i, 1)]).then_inc(th, 1)
                e.wait_ge(t_in, n)
                sc.activation(RT[:], RT[:], ACT.Sqrt, scale=-1.0).then_inc(mu, 1)
                e.wait_ge(evac, ph.group(i, 5) + 1 + BANK_CREDIT)
                sc.activation(GA[:], GA[:], ACT.Gelu_apprx_tanh).then_inc(ga, 1)
                e.wait_ge(oa, n)
                sc.activation(part(act, i * 2, 0), HH[:], ACT.Copy).then_inc(act_hi, 1)
                e.wait_ge(s_done, n * (UNITS + 1))
                e.dma_start(o["p_b_S"][0, 0, ds(i, 1)].rearrange("a k v -> k (a v)"), SR[:, PCH % 8, :]).then_inc(s_out, 16)
                e.dma_start(o["s_b_S"][0, :, ds(i, 1)].rearrange("s a k v -> k s (a v)"), SS[:]).then_inc(s_out, 16)
                e.wait_ge(oinv, n)
                sc.activation(SB[:], SB[:], ACT.Sqrt).then_inc(osq, 1)
                e.wait_ge(ob, n)
                sc.activation(part(act, i * 2 + 1, 0), OB[:], ACT.Copy).then_inc(act_hi, 1)

            ph = PH["wout"]
            with e.Fori(0, ph.bodies) as i:
                for j in range(4):
                    round_tile(ph, i, j)
                    if j % 2:
                        hi_of_x(ph, i, j // 2, COL["g_ffn"], i * 2 + j // 2)

            def store_rows(src, parts, dst_p, dst_s):
                for q, r0, n, whose, to in parts:
                    dst = dst_p if whose == "p" else dst_s
                    e.dma_start(dst[to:to + n], src[r0:r0 + n, q, :]).then_inc(out_dma, 16)

            for q in range(3):
                w = (P, 216 - P, 72)[q]
                e.wait_ge(nc_t, q + 1)
                sc.activation(orow[0:w, q, :], BM[q % 2][0:w, 0:P], ACT.Copy).then_inc(nc_c, 1)
            e.wait_ge(nc_c, 3)
            store_rows(orow, conv_row_parts(216, 24), o["p_a_conv"][0].rearrange("s r (c p) -> (s r c) p", p=P),
                       o["s_a_conv"][0].rearrange("s r (c p) -> (s r c) p", p=P))
            e.dma_start(o["p_a_h"][0].rearrange("s (c p) -> (s c) p", p=P), orow[0:8, 2, :]).then_inc(out_dma, 16)
            e.dma_start(o["s_a_h"][0].rearrange("s (c p) -> (s c) p", p=P), orow[8:72, 2, :]).then_inc(out_dma, 16)

            def ffn(l, gnext):
                for q in range(6):
                    w = min(P, 688 - q * P)
                    e.wait_ge(sf_t, l * 6 + q + 1)
                    sc.activation(SF.rearrange("p a f -> p (a f)")[:, q * P:q * P + w], BM[q % 2][:, 0:w], ACT.Copy).then_inc(sf_c, 1)
                norm_root(NORMS[f"up{l}0"])
                for p, (f0, n) in enumerate(PARTS):
                    ph = PH[f"up{l}{p}"]
                    cc = l * FFC + f0
                    with e.Fori(0, n) as i:
                        for j in range(4):
                            round_tile(ph, i, j)
                            if j == 1:
                                e.wait_ge(up_in, i + (cc + 1))
                                sc.activation(CV[:, 0:UPW - 2], UP[:, 2:UPW], ACT.Identity,
                                              scale=dcol("conv_f_w", i, (l * 3 + 2) * FFC + f0),
                                              bias=dcol("conv_f_b", i, l * FFC + f0)).then_inc(cv0, 1)
                            if j == 2:
                                e.wait_ge(cv2, i + (cc + 1))
                                sc.activation(CV[:, 0:UPW - 2], CV[:, 0:UPW - 2], ACT.Gelu_apprx_tanh).then_inc(gelu, 1)
                            if j == 3:
                                e.wait_ge(prod, i + (cc + 1))
                                sc.activation(part(act, i, 0), AC[:], ACT.Copy).then_inc(act_hi, 1)
                    ph = PH[f"down{l}{p}"]
                    last = p == len(PARTS) - 1
                    with e.Fori(0, ph.bodies - (last and l == 1)) as i:
                        for j in range(4):
                            round_tile(ph, i, j)
                            if last and gnext is not None and j % 2:
                                hi_of_x(ph, i, j // 2, gnext, i * 2 + j // 2)
                e.wait_ge(out_dma, 16 * (STORES_A if l == 0 else STORES_A + STORES_F + STORES_C))
                for q in range(7):
                    w = min(P, 774 - q * P)
                    e.wait_ge(nc_t, 3 + l * 7 + q + 1)
                    sc.activation(orow[0:w, q, :], BM[q % 2][0:w, 0:P], ACT.Copy).then_inc(nc_c, 1)
                e.wait_ge(nc_c, 3 + l * 7 + 7)
                store_rows(orow, conv_row_parts(774, 86), o["p_f_conv"][l].rearrange("s r (c p) -> (s r c) p", p=P),
                           o["s_f_conv"][l].rearrange("s r (c p) -> (s r c) p", p=P))

            ffn(0, COL["g_mix"] + DC)
            norm_root(NORMS["win"])
            e.wait_ge(a5v, 1)
            sc.activation(r5[:, 3, 0:2], r5[:, 2, 0:2], ACT.Exp).then_inc(a5a, 1)
            e.wait_ge(a5v, 2)
            sc.activation(r5[:, 6, :], r5[:, 5, :], ACT.Exp).then_inc(a5a, 1)
            e.wait_ge(a5v, 3)
            sc.activation(r5[:, 10, :], r5[:, 9, :], ACT.Sin)
            sc.activation(r5[:, 11, :], r5[:, 9, :], ACT.Sin, scale=0.5).then_inc(a5a, 1)
            ph = PH["win"]
            with e.Fori(0, ph.bodies) as i:
                for j in range(4):
                    round_tile(ph, i, j)
            for k in range(PAIRS):
                e.wait_ge(x5, 2 * k + 1)
                sc.activation(xs[:, 0, k, :], (BA if k % 2 == 0 else BM)[0][:, 0:T], ACT.Copy).then_inc(x5a, 1)
            for s in range(9):
                e.wait_ge(fs_t, s + 1)
                sc.activation(io5o[:, s, :], BM[s % 2][0:2 * PAIRS, 0:P], ACT.Copy).then_inc(fs_c, 1)
            e.wait_ge(fs_c, 9)
            for r, (np_, ns_) in enumerate((("p_c_re", "s_c_re"), ("p_c_im", "s_c_im"))):
                e.dma_start(o[np_][0, 0].rearrange("(q g) p -> q (g p)", g=2), io5o[32 * r:32 * r + 32, 0, :]).then_inc(out_dma, 16)
                e.dma_start(o[ns_][0].rearrange("s (q g) p -> q s (g p)", g=2), io5o[32 * r:32 * r + 32, 1:9, :]).then_inc(out_dma, 16)
            for c in range(8):
                e.wait_ge(y5v, c + 1)
                sc.activation(ys5[:, c % 2], ys5[:, c % 2], ACT.Gelu_apprx_tanh).then_inc(y5g, 1)
                e.wait_ge(y5g, c + 1)
                sc.activation(act[:, c, 0, :], ys5[:, c % 2], ACT.Copy).then_inc(act_hi, 1)

            ph = PH["glu"]
            with e.Fori(0, ph.bodies) as i:
                for j in range(4):
                    round_tile(ph, i, j)
                    if j % 2:
                        e.wait_ge(used, ph.tile(i, j) + 1 + CREDIT)
                        sc.activation(GS[:], bank[j][:, 0:T], ACT.Sigmoid).then_inc(gsig, 1)
                        hi_of_x(ph, i, j, COL["g_ffn"] + DC, i * 2 + j // 2)
            ffn(1, None)
            norm_root(NORMS["final"])
            e.wait_ge(out_dma, 16 * (STORES_A + 2 * STORES_F + STORES_C))
            for c in range(DC):
                e.wait_ge(y_t, c + 1)
                sc.activation(yo[:, 0:2, c * P:(c + 1) * P], bank[c % 2][:, 0:256].rearrange("p (a n) -> p a n", a=2), ACT.Copy)
                sc.activation(yo[0:64, 2, c * P:(c + 1) * P], bank[c % 2][0:64, 256:384], ACT.Copy).then_inc(y_c, 1)
                if c % 4 == 3:
                    c0, c1 = (c - 3) * P, (c + 1) * P
                    e.wait_ge(y_c, c + 1)
                    e.dma_start(o["y_prompt"][0, 0:P, c0:c1], yo[:, 0, c0:c1]).then_inc(out_dma, 16)
                    e.dma_start(o["y_prompt"][0, P:2 * P, c0:c1], yo[:, 1, c0:c1]).then_inc(out_dma, 16)
                    e.dma_start(o["y_sample"].rearrange("s t d -> (s t) d")[:, c0:c1], yo[0:64, 2, c0:c1]).then_inc(out_dma, 16)
            e.wait_ge(out_dma, 16 * (STORES_A + 2 * STORES_F + STORES_C + 12))
            e.wait_ge(s_out, 32 * HEADS + 16)

        @block.gpsimd
        def _(e):
            gp = nc.gpsimd
            st = Steps(e, pchain)

            def square(xc, first):
                if first:
                    gp.tensor_tensor(ssq[:], xc, xc, ALU.mult).then_inc(ssq_added, 1)
                else:
                    st.then(gp.tensor_tensor(sq[:], xc, xc, ALU.mult))
                    gp.tensor_tensor(ssq[:], ssq[:], sq[:], ALU.add).then_inc(ssq_added, 1)

            for c in range(DC):
                e.wait_ge(x_c, c + 1)
                if c:
                    e.wait_ge(ssq_added, c)
                square(X[:, c, :], c == 0)
            e.wait_ge(once, 1)

            with e.Fori(0, HEADS) as i:
                n = i + 1
                e.wait_ge(s_out, i * 32 + 16)
                e.dma_start(SS[:], a["state_b_S"][0, :, ds(i, 1)].rearrange("s a k v -> k s (a v)")).then_inc(ss_in, 16)
                e.dma_start(WR[:, 0, :], a["w_ra"][0, ds(i, 1)].rearrange("a k n -> k (a n)")).then_inc(wr_in, 16)
                e.dma_start(WR[:, 1, :], a["w_ia"][0, ds(i, 1)].rearrange("a k n -> k (a n)")).then_inc(wr_in, 16)
                st.enter(i, POOL_HEAD)
                e.wait_ge(bandin, n)
                for d in range(CH):
                    """G_d[t] = k[t-d] * f[t-d+1] ... f[t]; its product with q summed over k's features is the
                    attention of token t to token t-d."""
                    w = CH - d
                    if d == 1:
                        st.then(gp.tensor_tensor(bands(GG[:, 1, :], 1), bands(FM, 1), bands(K, 0)[:, :, 0:CH - 1], ALU.mult))
                    elif d > 1:
                        st.then(gp.tensor_tensor(bands(GG[:, d % 2, :], d), bands(FM, d),
                                                 bands(GG[:, (d - 1) % 2, :], d - 1)[:, :, 0:w], ALU.mult))
                    e.wait_ge(a_ready, i * CH + (d + 1))
                    gp.tensor_tensor(PB[:, d % 2, 0:NCH * w].rearrange("p (c w) -> p c w", w=w), bands(Q, d),
                                     bands(K, 0) if d == 0 else bands(GG[:, d % 2, :], d), ALU.mult).then_inc(p_ready, 1)
                    if d == 1:
                        e.wait_ge(sfx, n)
                        for par in range(2):
                            v = lambda t: t.rearrange("p (c q w) -> p c q w", q=2, w=CH)[:, :, par, :]
                            gp.tensor_tensor(v(KM[:, par, :]), v(K[:, 0:256]), v(FZ[:, 0:256]), ALU.mult)
                        for m in range(4):
                            nb = 3 if m < 2 else 2
                            for b in range(nb):
                                c0 = 32 * b + 8 * m
                                ins = gp.tensor_tensor(KM3[:, m, c0:c0 + 8], K[:, 256 + c0:264 + c0], FZ[:, 256 + c0:264 + c0], ALU.mult)
                        ins.then_inc(km, 1)
                e.wait_ge(gates_read, n)
                st.then(gp.tensor_tensor(IG[:], IG[:], XC[:], ALU.mult))
                e.wait_ge(mu, n)
                gp.tensor_tensor(IG[:, 1:T], IG[:, 1:T], RT[:, 1:T], ALU.mult).then_inc(b_ready, 1)
                st.leave(HEADS)

            def squares(ph, groups, norm):
                e.wait_ge(ms_done, norm)
                st.then(gp.memset(ssq[:], 0.0))
                with e.Fori(0, ph.bodies) as i:
                    st.enter(i, 2)
                    for r in range(2):
                        e.wait_ge(evac, ph.group(i, groups[r]) + 1 + BANK_CREDIT)
                        e.wait_ge(ssq_added, i * 2 + (norm * DC + r))
                        square(one(X, i * 2 + r), False)
                    st.leave(ph.bodies)

            def load_past(l):
                src = a["state_ffn_conv"][l].rearrange("s r (c p) -> (s r c) p", p=P)
                for q in range(6):
                    w = min(P, 688 - q * P)
                    e.dma_start(srow[0:w, q, :], src[q * P:q * P + w]).then_inc(sf_in, 16)

            e.wait_ge(act_lo, 2 * HEADS)
            e.wait_ge(s_out, 32 * HEADS + 16)
            load_past(0)
            squares(PH["wout"], (0, 1), 1)
            squares(PH["down02"], (0, 1), 2)
            e.wait_ge(evac, PH["win"].group(0, 0) + BANK_CREDIT)
            e.dma_start(r5[:, 0, :], a["lam_re"][0].rearrange("(q g) p -> q (g p)", g=2)).then_inc(in5, 16)
            e.dma_start(r5[:, 1, :], a["lam_im"][0].rearrange("(q g) p -> q (g p)", g=2)).then_inc(in5, 16)
            e.dma_start(r5[:, 2, 0:2], a["log_dt"][0].rearrange("(q g) -> q g", g=2)).then_inc(in5, 16)
            for r, n in enumerate(("bmat_re", "bmat_im")):
                e.dma_start(Bn[:, r], a[n][0].rearrange("(q g) p c -> (g p) q c", g=2)).then_inc(in5, 16)
            for r, n in enumerate(("cmat_re", "cmat_im")):
                e.dma_start(CN[:, r], a[n][0].rearrange("(j g) c p -> (g c) j p", g=8)).then_inc(in5, 16)
            for r, n in enumerate(("state_c_re", "state_c_im")):
                e.dma_start(io5[32 * r:32 * r + 32], a[n][0].rearrange("s (q g) p -> q s (g p)", g=2)).then_inc(in5, 16)
            e.wait_ge(y5v, 8)
            e.wait_ge(out_dma, 16 * (STORES_A + STORES_F + STORES_C))
            load_past(1)
            squares(PH["glu"], (1, 3), 3)
            squares(PH["down12"], (0, 1), 4)

        @block.vector
        def _(e):
            v = nc.vector
            st = Steps(e, dchain)

            def split_tile(ph, i, j):
                e.wait_ge(rounded, ph.tile(i, j) + 1 + RING)
                v.tensor_tensor(wl[:, j % RING, :], raw[:, j % RING, :], wh[:, j % RING, :].bitcast(F32), ALU.subtract) \
                    .then_inc(split, 1)

            def multiplied(ph, i, j):
                e.wait_ge(used, ph.tile(i, j) + 1 + CREDIT)

            def lo_of_x(c, g, hn):
                e.wait_ge(h_hi, hn)
                hi = part(h, c, 0).bitcast(F32)
                v.scalar_tensor_tensor(out=part(h, c, 1), in0=one(X, c), scalar=prm[:, ds(c + g, 1)], in1=hi,
                                       op0=ALU.mult, op1=ALU.subtract).then_inc(h_lo, 1)

            def norm_inverse(n):
                e.wait_ge(ms_done, n + 1)
                st.then(v.tensor_scalar(rs[:], BO[:, 0:T], 1.0 / D, EPS, ALU.mult, ALU.add))
                v.reciprocal(rs[:], rs[:]).then_inc(ms_inv, 1)
                e.wait_ge(rstd, n + 1)

            v.memset(tiny[:, 11, 0:1], 0.0).then_inc(split, CREDIT)
            v.memset(tiny[:, 11, 1:2], 0.0).then_inc(used, CREDIT)
            v.memset(tiny[:, 11, 2:3], 0.0).then_inc(evac, BANK_CREDIT)
            v.memset(tiny[:, 11, 3:4], 0.0).then_inc(a_ready, 2)
            v.memset(tiny[:, 11, 4:5], 0.0).then_inc(a_used, 2)
            v.memset(tiny[:, 11, 5:6], 0.0).then_inc(s_out, 16)
            v.memset(ones[:], 1.0)
            for c in range(DC):
                e.wait_ge(x_t, c + 1)
                v.tensor_copy(X[:, c, :], bank[c % 2][:, 0:T]).then_inc(x_c, 1)
            e.wait_ge(rows_t, 9)
            e.wait_ge(x_t, DC)
            v.memset(XA[:, 0:3], 0.0)
            v.memset(D1[:], 0.0)
            st.then(v.memset(EN[:], 0.0))
            v.memset(EN[:, CH - 1:TP:CH], 1.0)
            v.memset(EN[:, TP + LS - 1:T:LS], 1.0)
            v.memset(KM[:], 0.0)
            v.memset(KM3[:], 0.0)
            v.memset(FM[:, T:T + 1], 0.0).then_inc(once, 1)
            for c in range(DC):
                e.wait_ge(h_hi, c + 1)
                v.scalar_tensor_tensor(out=h[:, c, 1, :], in0=X[:, c, :], scalar=col("g_mix", c), in1=h[:, c, 0, :].bitcast(F32),
                                       op0=ALU.mult, op1=ALU.subtract).then_inc(h_lo, 1)
            lam = prm[:, COL["lam_a"]:COL["lam_a"] + HEADS]
            lb = prm[:, COL["lb"]:COL["lb"] + HEADS]
            e.wait_ge(rows_c, 9)
            st.then(v.scalar_tensor_tensor(out=tiny[:, 3, :], in0=lam, scalar=-1.0, in1=lam, op0=ALU.mult, op1=ALU.max))
            v.tensor_tensor(tiny[:, 5, :], lb, lb, ALU.subtract).then_inc(lam_v, 1)
            e.wait_ge(lam_a, 1)
            st.then(v.tensor_scalar(tiny[:, 7, :], tiny[:, 4, :], 2.0, None, ALU.add))
            st.then(v.reciprocal(tiny[:, 7, :], tiny[:, 7, :]))
            st.then(v.tensor_tensor(tiny[:, 7, :], tiny[:, 7, :], tiny[:, 4, :], ALU.mult))
            st.then(v.tensor_tensor(tiny[:, 8, :], tiny[:, 7, :], tiny[:, 7, :], ALU.mult))
            st.then(v.tensor_scalar(tiny[:, 9, :], tiny[:, 8, :], 1.0 / 17, None, ALU.mult))
            for m in (15, 13, 11, 9, 7, 5, 3):
                st.then(v.scalar_tensor_tensor(out=tiny[:, 9, :], in0=tiny[:, 9, :], scalar=1.0 / m, in1=tiny[:, 8, :],
                                               op0=ALU.add, op1=ALU.mult))
            st.then(v.scalar_tensor_tensor(out=tiny[:, 9, :], in0=tiny[:, 9, :], scalar=1.0, in1=tiny[:, 7, :],
                                           op0=ALU.add, op1=ALU.mult))
            st.then(v.tensor_scalar(tiny[:, 10, :], lam, -1.0, 0.0, ALU.mult, ALU.max))
            st.then(v.scalar_tensor_tensor(out=tiny[:, 9, :], in0=tiny[:, 9, :], scalar=2.0, in1=tiny[:, 10, :],
                                           op0=ALU.mult, op1=ALU.add))
            st.then(v.tensor_scalar(rate, tiny[:, 9, :], -C_RG, None, ALU.mult))
            st.then(v.reciprocal(tiny[:, 5, :], tiny[:, 6, :]))
            st.then(v.tensor_tensor(tiny[:, 5, :], tiny[:, 5, :], tiny[:, 6, :], ALU.mult))
            st.then(v.tensor_tensor(tiny[:, 5, :], tiny[:, 5, :], tiny[:, 5, :], ALU.subtract))
            st.then(v.tensor_scalar(tiny[:, 5, :], tiny[:, 5, :], 0.0, 1.0, ALU.max, ALU.min))
            st.then(v.tensor_scalar(lbm, tiny[:, 5, :], 1e-30, None, ALU.max))
            st.then(v.tensor_scalar(oml, tiny[:, 5, :], -1.0, 1.0, ALU.mult, ALU.add))
            for j in range(RING):
                e.wait_ge(rounded, j + 1)
                v.tensor_tensor(wl[:, j, :], raw[:, j, :], wh[:, j, :].bitcast(F32), ALU.subtract).then_inc(split, 1)
            norm_inverse(0)

            ph = PH["head"]
            with e.Fori(0, HEADS) as i:
                st.enter(i, DVE_HEAD)
                n = i + 1
                own = {"d": 0}

                def take(dst, r):
                    multiplied(ph, i, 2 * r + 1)
                    v.tensor_tensor(dst, bank[ph.bank(r)][:, 0:T], rs[:], ALU.mult).then_inc(evac, 1)
                    e.wait_ge(evac, ph.group(i, r) + 1 + BANK_CREDIT)

                def band(d):
                    w = CH - d
                    e.wait_ge(a_ready, i * CH + (d + 3))
                    wt = BA[d % 2][:, 0:NCH * w].rearrange("p (c w) -> p c w", w=w)
                    vals = bands(V, 0)[:, :, 0:w]
                    if d == 0:
                        v.tensor_tensor(bands(OB, 0), wt, vals, ALU.mult).then_inc(a_used, 1)
                        e.wait_ge(a_used, i * CH + (d + 3))
                    else:
                        v.tensor_tensor(W[:, 0:NCH * w].rearrange("p (c w) -> p c w", w=w), wt, vals, ALU.mult).then_inc(a_used, 1)
                        e.wait_ge(a_used, i * CH + (d + 3))
                        st.then(v.tensor_tensor(bands(OB, d), bands(OB, d), W[:, 0:NCH * w].rearrange("p (c w) -> p c w", w=w), ALU.add))

                for j in range(12):
                    split_tile(ph, i, j)
                    if j == 1:
                        take(Q[:], 0)
                    if j == 3:
                        take(FZ[:], 1)
                        e.wait_ge(sk, n)
                        st.then(v.tensor_scalar(FM[:, 0:T], FM[:, 0:T], tiny[:, 2, ds(i, 1)], tiny[:, 1, ds(i, 1)], ALU.mult, ALU.add))
                        st.then(v.tensor_scalar(K[:], K[:], tiny[:, 2, ds(i, 1)], None, ALU.mult))
                        v.tensor_copy(D1[:, 0:TP:CH], FM[:, 0:TP:CH])
                        st.then(v.tensor_copy(D1[:, TP:T:LS], FM[:, TP:T:LS]))
                        v.memset(FM[:, 0:TP:CH], 0.0)
                        v.memset(FM[:, TP:T:LS], 0.0).then_inc(bandin, 1)
                        e.wait_ge(bandin, n)
                        st.then(v.tensor_tensor_scan(QF[:], FM[:, 0:T], D1[:], 0.0, ALU.mult, ALU.add))
                        v.tensor_tensor_scan(FZ[:, ::-1], FM[:, 1:T + 1][:, ::-1], EN[:, ::-1], 0.0, ALU.mult, ALU.add).then_inc(sfx, 1)
                        v.tensor_copy(FE[:, 0:PCH], QF[:, CH - 1:TP:CH])
                        st.then(v.tensor_copy(FE[:, PCH:UNITS], QF[:, TP + LS - 1:T:LS]))
                        st.then(v.tensor_tensor(QF[:], QF[:], Q[:], ALU.mult))
                    if j == 5:
                        take(V[:], 2)
                    if j == 7:
                        multiplied(ph, i, 7)
                        pv = bank[ph.bank(3)][:, 0:T]
                        v.tensor_tensor(XA[:, 3:3 + TP], pv[:, 0:TP], rs[:, 0:TP], ALU.mult)
                        v.tensor_tensor(XAs[:, :, 3:3 + LS], samples(pv), samples(rs), ALU.mult).then_inc(evac, 1)
                        past = prm[:, COL["a_conv"]:COL["a_conv"] + 192].rearrange("p (s r c) -> p s r c", r=3, c=HEADS)
                        v.tensor_copy(XAs[:, :, 0:3], past[:, :, :, ds(i, 1)].rearrange("p s r c -> p s (r c)")).then_inc(conv_in, 1)
                        e.wait_ge(conv_in, n)
                        v.tensor_copy(ncva[:, 0, :, ds(i, 1)].rearrange("p r c -> p (r c)"), XA[:, TP:TP + 3])
                        v.tensor_copy(ncva[:, 1:1 + NS, :, ds(i, 1)].rearrange("p s r c -> p s (r c)"), XAs[:, :, LS:LS + 3])
                        e.wait_ge(ct, n)
                        for k in (2, 1):
                            st.then(v.scalar_tensor_tensor(out=CT[:, 0:360], in0=XA[:, k:k + 360], scalar=dcol("conv_a_w", i, 8 * k),
                                                           in1=CT[:, 0:360], op0=ALU.mult, op1=ALU.add))
                        v.scalar_tensor_tensor(out=XC[:, 0:TP], in0=XA[:, 0:TP], scalar=dcol("conv_a_w", i), in1=CT[:, 0:TP],
                                               op0=ALU.mult, op1=ALU.add)
                        v.scalar_tensor_tensor(out=samples(XC), in0=XAs[:, :, 0:LS], scalar=dcol("conv_a_w", i),
                                               in1=CTs[:, :, 0:LS], op0=ALU.mult, op1=ALU.add).then_inc(xc, 1)
                    if j == 9:
                        take(GB[:], 4)
                    for d in {6: (0,), 7: (1, 2), 8: (3, 4), 9: (5, 6, 7), 10: (8, 9, 10), 11: tuple(range(11, CH))}.get(j, ()):
                        band(d)
                    if j == 9:
                        e.wait_ge(sbg, n)
                        st.then(v.scalar_tensor_tensor(out=GB[:], in0=GB[:], scalar=dcol("gn_b", i), in1=SB[:],
                                                       op0=ALU.mult, op1=ALU.mult))
                    if j == 10:
                        e.wait_ge(th, n)
                        st.then(v.tensor_tensor(RT[:], AA[:], AA[:], ALU.mult))
                        v.scalar_tensor_tensor(out=RT[:], in0=RT[:], scalar=1.0, in1=CT[:, 0:T], op0=ALU.add, op1=ALU.mult) \
                            .then_inc(t_in, 1)
                take(GA[:], 5)

                e.wait_ge(s_out, i * 32 + 16)
                v.memset(SR[:, 0, :], 0.0).then_inc(s_done, 1)
                for u in range(UNITS):
                    e.wait_ge(s_done, i * (UNITS + 1) + (u + 1))
                    if u % 4 == 0:
                        e.wait_ge(u_ready, i * 7 + (u // 4 + 1))
                    if u < PCH:
                        old, new = SR[:, u % 8, :], SR[:, (u + 1) % 8, :]
                        if u >= 7:
                            e.wait_ge(inter, i * UNITS + (u - 6))
                    else:
                        old = new = SS[:, u - PCH, :]
                        e.wait_ge(inter, i * UNITS + (u + 1))
                    v.scalar_tensor_tensor(out=new, in0=old, scalar=FE[:, u:u + 1],
                                           in1=BM[u // 4 % 2][:, u % 4 * P:(u % 4 + 1) * P], op0=ALU.mult, op1=ALU.add) \
                        .then_inc(s_done, 1)
                e.wait_ge(inter, n * UNITS)
                st.then(v.tensor_tensor(OB[:], OB[:], BO[:, 0:T], ALU.add))
                v.tensor_tensor(W[:], OB[:], OB[:], ALU.mult).then_inc(oo, 1)

                e.wait_ge(b_ready, n)
                h0 = prm[:, COL["a_h"]:COL["a_h"] + 64].rearrange("p (s c) -> p s c", c=HEADS)[:, :, ds(i, 1)].rearrange("p s c -> p (s c)")
                st.then(v.tensor_tensor(HH[:, 0:NS], AA[:, TP:T:LS], h0, ALU.mult))
                st.then(v.tensor_tensor(IG[:, TP:T:LS], IG[:, TP:T:LS], HH[:, 0:NS], ALU.add))
                st.then(v.memset(AA[:, TP:T:LS], 0.0))
                st.then(v.tensor_tensor_scan(HH[:], AA[:], IG[:], 0.0, ALU.mult, ALU.add))
                v.tensor_copy(hlast[:, 0, ds(i, 1)], HH[:, TP - 1:TP])
                st.then(v.tensor_copy(hlast[:, 1:1 + NS, ds(i, 1)].rearrange("p s c -> p (s c)"), HH[:, TP + LS - 1:T:LS]))
                e.wait_ge(ga, n)
                v.tensor_tensor(HH[:], HH[:], GA[:], ALU.mult).then_inc(oa, 1)

                e.wait_ge(oms, n)
                st.then(v.tensor_scalar(SB[:], BM[1][:, 0:T], 1.0 / P, EPS, ALU.mult, ALU.add))
                v.reciprocal(SB[:], SB[:]).then_inc(oinv, 1)
                e.wait_ge(act_hi, i * 2 + 1)
                v.tensor_tensor(part(act, i * 2, 1), HH[:], part(act, i * 2, 0).bitcast(F32), ALU.subtract).then_inc(act_lo, 1)
                e.wait_ge(osq, n)
                st.then(v.tensor_tensor(OB[:], OB[:], SB[:], ALU.mult))
                v.tensor_tensor(OB[:], OB[:], GB[:], ALU.mult).then_inc(ob, 1)
                e.wait_ge(act_hi, i * 2 + 2)
                v.tensor_tensor(part(act, i * 2 + 1, 1), OB[:], part(act, i * 2 + 1, 0).bitcast(F32), ALU.subtract).then_inc(act_lo, 1)
                st.leave(HEADS)

            def add_to_x(ph, i, r, j, g, norm):
                c = i * 2 + r
                multiplied(ph, i, j)
                v.tensor_tensor(one(X, c), one(X, c), bank[ph.bank(r)][:, 0:T], ALU.add).then_inc(evac, 1)
                if g is not None:
                    lo_of_x(c, g, i * 2 + (norm * DC + r + 1))

            ph = PH["wout"]
            with e.Fori(0, ph.bodies) as i:
                for j in range(4):
                    split_tile(ph, i, j)
                    if j % 2:
                        add_to_x(ph, i, j // 2, j, COL["g_ffn"], 1)

            def ffn(l, gnext, norm_next):
                if l == 0:
                    e.wait_ge(nc_t, 3)
                e.wait_ge(s_out, 32 * HEADS + 16)
                v.memset(UP[:, 0:2], 0.0)
                norm_inverse(NORMS[f"up{l}0"])
                e.wait_ge(sf_c, 6 * (l + 1))
                for p, (f0, n) in enumerate(PARTS):
                    ph = PH[f"up{l}{p}"]
                    cc = l * FFC + f0
                    slots = 16 + l * 8 + cc
                    w = lambda i, k: dcol("conv_f_w", i, (l * 3 + k) * FFC + f0)
                    with e.Fori(0, n) as i:
                        st.enter(i, 1)
                        for j in range(4):
                            split_tile(ph, i, j)
                            if j == 1:
                                multiplied(ph, i, 1)
                                pv = bank[0][:, 0:T]
                                v.tensor_tensor(UP[:, 2:2 + TP], pv[:, 0:TP], rs[:, 0:TP], ALU.mult)
                                v.tensor_tensor(UPs[:, :, 2:2 + LS], samples(pv), samples(rs), ALU.mult).then_inc(evac, 1)
                                v.tensor_copy(UPs[:, :, 0:2], SF.rearrange("p (s r) f -> p s r f", r=2)[:, :, :, ds(i + f0, 1)]
                                              .rearrange("p s r f -> p s (r f)")).then_inc(up_in, 1)
                                e.wait_ge(up_in, i + (cc + 1))
                                v.tensor_copy(NCF[:, 0, :, ds(i + f0, 1)].rearrange("p r f -> p (r f)"), UP[:, TP:TP + 2])
                                v.tensor_copy(NCF[:, 1:1 + NS, :, ds(i + f0, 1)].rearrange("p s r f -> p s (r f)"), UPs[:, :, LS:LS + 2])
                                e.wait_ge(cv0, i + (cc + 1))
                                st.then(v.scalar_tensor_tensor(out=CV[:, 0:UPW - 2], in0=UP[:, 1:UPW - 1], scalar=w(i, 1),
                                                               in1=CV[:, 0:UPW - 2], op0=ALU.mult, op1=ALU.add))
                                v.scalar_tensor_tensor(out=CV[:, 0:UPW - 2], in0=UP[:, 0:UPW - 2], scalar=w(i, 0),
                                                       in1=CV[:, 0:UPW - 2], op0=ALU.mult, op1=ALU.add).then_inc(cv2, 1)
                            if j == 3:
                                multiplied(ph, i, 3)
                                v.tensor_tensor(GT[:], bank[1][:, 0:T], rs[:], ALU.mult).then_inc(evac, 1)
                                e.wait_ge(evac, ph.group(i, 1) + 1 + BANK_CREDIT)
                                e.wait_ge(gelu, i + (cc + 1))
                                v.tensor_tensor(AC[:, 0:TP], GT[:, 0:TP], CV[:, 0:TP], ALU.mult)
                                v.tensor_tensor(samples(AC), samples(GT), CVs[:, :, 0:LS], ALU.mult).then_inc(prod, 1)
                                e.wait_ge(prod, i + (cc + 1))
                                e.wait_ge(act_hi, i + (slots + 1))
                                v.tensor_tensor(part(act, i, 1), AC[:], part(act, i, 0).bitcast(F32), ALU.subtract).then_inc(act_lo, 1)
                        st.leave(n)
                    ph = PH[f"down{l}{p}"]
                    last = p == len(PARTS) - 1
                    g = gnext if last else None
                    end = last and l == 1
                    with e.Fori(0, ph.bodies - end) as i:
                        for j in range(4):
                            split_tile(ph, i, j)
                            if j % 2:
                                add_to_x(ph, i, j // 2, j, g, norm_next)
                    if end:
                        for r in range(2):
                            add_to_x(ph, ph.bodies - 1, r, 2 * r + 1, None, norm_next)
                v.tensor_copy(NCF[:, 0, 0, 0:1], NCF[:, 0, 0, 0:1]).then_inc(nc_v, 1)

            ffn(0, COL["g_mix"] + DC, 2)
            norm_inverse(NORMS["win"])

            R = lambda k: r5[:, k, :]
            e.wait_ge(in5, 16 * 9)
            v.memset(BX[:], 0.0)
            v.tensor_copy(r5[:, 14, 0:1], r5[:, 2, 0:1]).then_inc(a5v, 1)
            e.wait_ge(a5a, 1)
            for g in range(2):
                sl = slice(g * P5, (g + 1) * P5)
                v.tensor_scalar(r5[:, 5, sl], r5[:, 0, sl], r5[:, 3, g:g + 1], None, ALU.mult)
                ins = v.tensor_scalar(r5[:, 7, sl], r5[:, 1, sl], r5[:, 3, g:g + 1], None, ALU.mult)
            ins.then_inc(a5v, 1)
            e.wait_ge(a5v, 2)
            magic = 1.5 * 2.0 ** 23
            st.then(v.tensor_scalar(R(8), R(7), float(1 / (2 * np.pi)), magic, ALU.mult, ALU.add))
            st.then(v.tensor_scalar(R(8), R(8), magic, None, ALU.subtract))
            c1 = 6.28125
            c2 = float(np.float32(np.round((2 * np.pi - c1) * 2 ** 21) / 2 ** 21))
            c3 = float(2 * np.pi - c1 - c2)
            st.then(v.scalar_tensor_tensor(out=R(9), in0=R(8), scalar=-c1, in1=R(7), op0=ALU.mult, op1=ALU.add))
            st.then(v.scalar_tensor_tensor(out=R(9), in0=R(8), scalar=-c2, in1=R(9), op0=ALU.mult, op1=ALU.add))
            st.then(v.scalar_tensor_tensor(out=R(9), in0=R(8), scalar=-c3, in1=R(9), op0=ALU.mult, op1=ALU.add))
            pi = float(np.nextafter(np.float32(np.pi), np.float32(0)))
            v.tensor_scalar(R(9), R(9), pi, -pi, ALU.min, ALU.max).then_inc(a5v, 1)
            e.wait_ge(a5a, 3)
            st.then(v.tensor_tensor(R(11), R(11), R(11), ALU.mult))
            st.then(v.tensor_scalar(R(11), R(11), -2.0, 1.0, ALU.mult, ALU.add))
            st.then(v.tensor_tensor(R(12), R(6), R(11), ALU.mult))
            st.then(v.tensor_tensor(R(13), R(6), R(10), ALU.mult))
            st.then(v.tensor_tensor(R(14), R(0), R(0), ALU.mult))
            st.then(v.tensor_tensor(R(15), R(1), R(1), ALU.mult))
            st.then(v.tensor_tensor(R(14), R(14), R(15), ALU.add))
            st.then(v.reciprocal(R(14), R(14)))
            st.then(v.scalar_tensor_tensor(out=R(8), in0=R(12), scalar=-1.0, in1=R(0), op0=ALU.add, op1=ALU.mult))
            st.then(v.tensor_tensor(R(9), R(13), R(1), ALU.mult))
            st.then(v.tensor_tensor(R(8), R(8), R(9), ALU.add))
            st.then(v.tensor_tensor(R(8), R(8), R(14), ALU.mult))
            st.then(v.tensor_tensor(R(9), R(13), R(0), ALU.mult))
            st.then(v.scalar_tensor_tensor(out=R(10), in0=R(12), scalar=-1.0, in1=R(1), op0=ALU.add, op1=ALU.mult))
            st.then(v.tensor_tensor(R(9), R(9), R(10), ALU.subtract))
            v.tensor_tensor(R(9), R(9), R(14), ALU.mult).then_inc(a5v, 1)
            for r in range(2):
                for g in range(2):
                    ins = v.tensor_scalar(CX[:, r].rearrange("p j (g x) -> p j g x", g=2)[:, :, g, :], CN[:, r],
                                          masks[:, 2 * r + g:2 * r + g + 1], None, ALU.mult)
            ins.then_inc(a5v, 1)

            e.wait_ge(out_dma, 16 * (STORES_A + STORES_F))
            ph = PH["win"]
            with e.Fori(0, ph.bodies) as i:
                for j in range(4):
                    split_tile(ph, i, j)
                    if j % 2:
                        multiplied(ph, i, j)
                        v.tensor_tensor(one(U5, i * 2 + j // 2), bank[ph.bank(j // 2)][:, 0:T], rs[:], ALU.mult).then_inc(evac, 1)

            e.wait_ge(t5, 1)
            az = BM[0][:, 0:4 * PAIRS].rearrange("p (k n) -> p k n", k=4)
            v.tensor_copy(A5[:, 0, 0, :], az[:, 0, :])
            v.tensor_copy(A5[:, 0, 1, :], az[:, 0, :])
            v.tensor_scalar(A5[:, 1, 0, :], az[:, 1, :], -1.0, None, ALU.mult)
            v.tensor_copy(A5[:, 1, 1, :], az[:, 1, :])
            v.tensor_copy(zz[:, 0:2, :], az[:, 2:4, :]).then_inc(c5, 1)
            e.wait_ge(c5, 1)
            zb = lambda k: zz[:, k, :].unsqueeze(2).to_broadcast([P, PAIRS, C5])
            v.tensor_tensor(B2[:, 0], Bn[:, 0], zb(0), ALU.mult)
            st.then(v.tensor_tensor(B2[:, 1], Bn[:, 1], zb(1), ALU.mult))
            st.then(v.tensor_tensor(B2[:, 0], B2[:, 0], B2[:, 1], ALU.subtract))
            st.then(v.tensor_tensor(B2[:, 1], Bn[:, 1], zb(0), ALU.mult))
            st.then(v.tensor_tensor(Bn[:, 0], Bn[:, 0], zb(1), ALU.mult))
            st.then(v.tensor_tensor(B2[:, 1], B2[:, 1], Bn[:, 0], ALU.add))
            for r in range(2):
                for g in range(2):
                    rowsl = slice(g * P5, (g + 1) * P5)
                    ins = v.tensor_copy(BX[rowsl, r].rearrange("p j (q g c) -> p (j q) g c", q=4, g=2)[:, :, g, :], B2[rowsl, r])
            ins.then_inc(a5v, 1)
            for b in range(8):
                dst = (CTm if b < 4 else BTm)[:, b % 2 * 4:b % 2 * 4 + 4, b % 4 // 2, :]
                e.wait_ge(t5, b + 2)
                v.tensor_copy(dst, BM[(b + 1) % 2][:].rearrange("p (j n) -> p j n", j=4)).then_inc(c5, 1)
            e.wait_ge(t5, 10)
            v.tensor_copy(st5.rearrange("p s r k -> p (s r k)"), BM[1][:]).then_inc(c5, 1)
            for k in range(PAIRS):
                e.wait_ge(x5, 2 * k + 2)
                v.tensor_copy(xs[:, 1, k, :], (BA if k % 2 == 0 else BM)[1][:, 0:T]).then_inc(x5v, 1)
            e.wait_ge(x5a, PAIRS)
            e.wait_ge(x5v, PAIRS)
            e.wait_ge(c5, 10)

            def step5(prev, cur, shape):
                if len(shape) == 3:
                    A = lambda k: A5[:, k].unsqueeze(3).to_broadcast([P, 2, PAIRS, NS])
                    m = lambda k: tmp5[:, k, :].rearrange("p (r q s) -> p r q s", r=2, q=PAIRS)
                else:
                    A = lambda k: A5[:, k]
                    m = lambda k: tmp5[:, k, 0:2 * PAIRS].rearrange("p (r q) -> p r q", r=2)
                v.tensor_tensor(m(0), A(0), prev, ALU.mult)
                v.tensor_tensor(m(1)[:, 0], A(1)[:, 0], prev[:, 1], ALU.mult)
                st.then(v.tensor_tensor(m(1)[:, 1], A(1)[:, 1], prev[:, 0], ALU.mult))
                st.then(v.tensor_tensor(m(0), m(0), m(1), ALU.add))
                st.then(v.tensor_tensor(cur, cur, m(0), ALU.add))

            xss = xs[:, :, :, TP:T].rearrange("p r q (s w) -> p r q s w", w=LS)
            s0 = st5.rearrange("p s r q -> p r q s")
            for w in range(LS):
                prev = s0 if w == 0 else xss[:, :, :, :, w - 1]
                step5(prev, xss[:, :, :, :, w], (2, PAIRS, NS))
            at = lambda t: xs[:, :, :, t]
            for t in range(1, 4):
                step5(at(t - 1), at(t), (2, PAIRS))
            dat = lambda i, k: xs[:, :, :, ds(i * 4 + k, 1)].rearrange("p r q a -> p r (q a)")
            with e.Fori(0, (TP - 4) // 4) as i:
                st.enter(i, 12)
                for k in range(4, 8):
                    step5(dat(i, k - 1), dat(i, k), (2, PAIRS))
                st.leave((TP - 4) // 4)
            v.tensor_copy(tmp5[:, 0, 0:1], tmp5[:, 1, 0:1]).then_inc(scan5, 1)
            for c in range(8):
                if c >= 2:
                    e.wait_ge(act_lo, 16 + FFC + c - 1)
                e.wait_ge(y5, c + 1)
                v.scalar_tensor_tensor(out=ys5[:, c % 2], in0=U5[:, c, :], scalar=col("d_skip", c), in1=BA[c % 2][:, 0:T],
                                       op0=ALU.mult, op1=ALU.add).then_inc(y5v, 1)
                e.wait_ge(act_hi, 16 + FFC + c + 1)
                v.tensor_tensor(act[:, c, 1, :], ys5[:, c % 2], act[:, c, 0, :].bitcast(F32), ALU.subtract).then_inc(act_lo, 1)

            ph = PH["glu"]
            with e.Fori(0, ph.bodies) as i:
                st.enter(i, 2)
                for j in range(4):
                    split_tile(ph, i, j)
                    if j % 2:
                        c = i * 2 + j // 2
                        e.wait_ge(gsig, i * 2 + (j // 2 + 1))
                        st.then(v.tensor_tensor(VT[:], bank[j - 1][:, 0:T], GS[:], ALU.mult))
                        v.tensor_tensor(one(X, c), one(X, c), VT[:], ALU.add).then_inc(evac, 2)
                        lo_of_x(c, COL["g_ffn"] + DC, i * 2 + (3 * DC + j // 2 + 1))
                st.leave(ph.bodies)
            ffn(1, None, 4)
            norm_inverse(NORMS["final"])
            for c in range(DC):
                if c >= 2:
                    e.wait_ge(y_t, c - 1)
                v.scalar_tensor_tensor(out=yg[:, c % 2, :], in0=X[:, c, :], scalar=col("g_final", c), in1=rs[:],
                                       op0=ALU.mult, op1=ALU.mult).then_inc(yg_done, 1)

        @block.tensor
        def _(e):
            pe = nc.tensor

            def tile(ph, i, j, kn, x, b, first, last):
                e.wait_ge(split, ph.tile(i, j) + 1 + CREDIT)
                slot, out = j % RING, bank[b][:, 0:T]
                for k in range(kn):
                    hi, lo = x(k)
                    whi, wlo = wh[:, slot, k * P:(k + 1) * P], wl[:, slot, k * P:(k + 1) * P]
                    pe.matmul(out, whi, hi, start=first and k == 0, stop=False)
                    pe.matmul(out, whi, lo, start=False, stop=False)
                    ins = pe.matmul(out, wlo, hi, start=False, stop=last and k == kn - 1)
                ins.then_inc(used, 1)

            def free(ph, i, r):
                e.wait_ge(evac, ph.group(i, r) + (1 + BANK_CREDIT - ph.banks))

            def from_h(k0):
                return lambda k: (h[:, k0 + k, 0, :], h[:, k0 + k, 1, :])

            def from_act(k0):
                return lambda k: (act[:, k0 + k, 0, :], act[:, k0 + k, 1, :])

            def mean_squares(n):
                e.wait_ge(ssq_added, (n + 1) * DC)
                pe.matmul(BO[:, 0:T], ones[:], ssq[:], start=True, stop=True).then_inc(ms_done, 1)

            e.wait_ge(consts_in, 32)
            e.wait_ge(rows_in, 16 * 18)
            for q in range(9):
                w = (80, 86, 86, 86, 86, 88, 64, 96, 96)[q]
                if q >= 2:
                    e.wait_ge(rows_c, q - 1)
                pe.transpose(BM[q % 2][:, 0:w], rows[0:w, q, :], ident[0:w, 0:w]).then_inc(rows_t, 1)
            e.wait_ge(x_in, 80)
            for c in range(DC):
                if c >= 2:
                    e.wait_ge(x_c, c - 1)
                for t in range(3):
                    n = (P, P, T - 2 * P)[t]
                    ins = pe.transpose(bank[c % 2][:, t * P:t * P + n], xin[0:n, t, c * P:(c + 1) * P], ident[0:n, 0:n])
                ins.then_inc(x_t, 1)
            e.wait_ge(once, 1)
            mean_squares(0)
            e.wait_ge(h_lo, DC)

            ph = PH["head"]
            with e.Fori(0, HEADS) as i:
                n = i + 1
                turns = [0]

                def band(d):
                    w = CH - d
                    e.wait_ge(p_ready, i * CH + (d + 1))
                    e.wait_ge(a_used, i * CH + (d + 1))
                    pe.matmul(BA[d % 2][:, 0:NCH * w], ones[:], PB[:, d % 2, 0:NCH * w], start=True, stop=True).then_inc(a_ready, 1)

                def updates(b):
                    if b < 2:
                        e.wait_ge(gates_read, n)
                    else:
                        e.wait_ge(s_done, i * (UNITS + 1) + (4 * (b - 2) + 5))
                    row = None
                    for u in range(4 * b, min(4 * b + 4, UNITS)):
                        out = BM[b % 2][:, u % 4 * P:(u % 4 + 1) * P]
                        if u < PCH - 1:
                            t, r0, vers = u // 8, 32 * (u % 8 // 2), [(u // 8) * 2 + u % 2]
                            rn = 32
                        else:
                            t, off = 2, (0 if u == PCH - 1 else CH + LS * (u - PCH))
                            r0, rn = off // 32 * 32, min(32, 80 - off // 32 * 32)
                            vers = [4, 5] if u == PCH - 1 else [4 + off % 32 // 8]
                        if row not in (None, r0):
                            ins.then_inc(row_turn, 1)
                            turns[0] += 1
                            e.wait_ge(row_turn, i * ROW_TURNS + turns[0])
                        row = r0
                        for m, k in enumerate(vers):
                            ins = pe.matmul(out, TK[r0:r0 + rn, k, :], TV[r0:r0 + rn, t, :], start=m == 0, stop=m == len(vers) - 1)
                    ins.then_inc(u_ready, 1)

                def with_state(us):
                    for u in us:
                        if u < PCH:
                            e.wait_ge(s_done, i * (UNITS + 1) + (u + 1))
                            c0, w, S = u * CH, CH, SR[:, u % 8, :]
                        else:
                            e.wait_ge(ss_in, n * 16)
                            c0, w, S = TP + (u - PCH) * LS, LS, SS[:, u - PCH, :]
                        pe.matmul(BO[:, c0:c0 + w], S, QF[:, c0:c0 + w], start=True, stop=True).then_inc(inter, 1)

                for j in range(12):
                    if j % 2 == 0:
                        free(ph, i, j // 2)
                    tile(ph, i, j, 8, from_h(8 * (j % 2)), ph.bank(j // 2), j % 2 == 0, j % 2 == 1)
                    for d in {6: (0,), 7: (1, 2), 8: (3, 4), 9: (5, 6, 7), 10: (8, 9, 10), 11: tuple(range(11, CH))}.get(j, ()):
                        band(d)
                    if j == 8:
                        e.wait_ge(km, n)
                        for k in range(4):
                            ins = pe.transpose(BM[0][:, k * P:(k + 1) * P], KM[:, k % 2, k // 2 * P:(k // 2 + 1) * P], ident[:])
                        ins.then_inc(kt, 1)
                        for k in range(4):
                            ins = pe.transpose(BM[1][0:80, k * P:(k + 1) * P], KM3[:, k, 0:80], ident[:])
                        ins.then_inc(kt, 1)
                        for k in range(3):
                            w = min(P, T - k * P)
                            ins = pe.transpose(BO[0:w, k * P:(k + 1) * P], V[:, k * P:k * P + w], ident[:])
                        ins.then_inc(kt, 1)
                    if j == 9:
                        e.wait_ge(tk_copied, i * 3 + 2)
                        e.wait_ge(xc, n)
                        e.wait_ge(wr_in, n * 32)
                        pe.matmul(BM[0][:, 0:T], WR[:, 0, :], XC[:], start=True, stop=True)
                        pe.matmul(BM[1][:, 0:T], WR[:, 1, :], XC[:], start=True, stop=True).then_inc(gates, 1)
                    if j == 10:
                        e.wait_ge(tk_copied, i * 3 + 3)
                        updates(0)
                        updates(1)
                for b in range(7):
                    with_state(range(4 * b, min(4 * b + 4, UNITS)))
                    if b + 2 < 7:
                        updates(b + 2)
                assert turns[0] == ROW_TURNS
                e.wait_ge(oo, n)
                pe.matmul(BM[1][:, 0:T], ones[:], W[:], start=True, stop=True).then_inc(oms, 1)

            mixed = lambda k0: (lambda k: (act[:, (2 * (k0 + k)) if k0 + k < 8 else (2 * (k0 + k - 8) + 1), 0, :],
                                           act[:, (2 * (k0 + k)) if k0 + k < 8 else (2 * (k0 + k - 8) + 1), 1, :]))
            e.wait_ge(act_lo, 2 * HEADS)
            ph = PH["wout"]
            with e.Fori(0, ph.bodies) as i:
                for j in range(4):
                    if j % 2 == 0:
                        free(ph, i, j // 2)
                    tile(ph, i, j, 8, mixed(8 * (j % 2)), ph.bank(j // 2), j % 2 == 0, j % 2 == 1)

            flatn = ncva.rearrange("p s r c -> p (s r c)")
            for q, src in enumerate((flatn[:, 0:P], flatn[:, P:216], hlast.rearrange("p s c -> p (s c)"))):
                if q == 2:
                    e.wait_ge(nc_c, 1)
                pe.transpose(BM[q % 2][0:src.shape[1], 0:P], src, ident[:]).then_inc(nc_t, 1)

            def ffn(l):
                e.wait_ge(sf_in, 16 * 6 * (l + 1))
                for q in range(6):
                    w = min(P, 688 - q * P)
                    if q >= 2 or l == 0:
                        e.wait_ge(sf_c, l * 6 + q - 1) if q >= 2 else e.wait_ge(nc_c, 3)
                    pe.transpose(BM[q % 2][:, 0:w], srow[0:w, q, :], ident[0:w, 0:w]).then_inc(sf_t, 1)
                mean_squares(NORMS[f"up{l}0"])
                e.wait_ge(h_lo, DC * (2 if l == 0 else 4))
                for p, (f0, n) in enumerate(PARTS):
                    ph = PH[f"up{l}{p}"]
                    with e.Fori(0, n) as i:
                        for j in range(4):
                            if j % 2 == 0:
                                free(ph, i, j // 2)
                            tile(ph, i, j, 8, from_h(8 * (j % 2)), ph.bank(j // 2), j % 2 == 0, j % 2 == 1)
                    e.wait_ge(act_lo, 16 + l * 8 + l * FFC + f0 + n)
                    ph = PH[f"down{l}{p}"]
                    with e.Fori(0, ph.bodies) as i:
                        for j in range(4):
                            k0, kn = halves(n)[j % 2]
                            if j % 2 == 0:
                                free(ph, i, j // 2)
                            tile(ph, i, j, kn, from_act(k0), ph.bank(j // 2), j % 2 == 0, j % 2 == 1)
                flat = NCF.rearrange("p s r f -> p (s r f)")
                e.wait_ge(nc_v, l + 1)
                for q in range(7):
                    w = min(P, 774 - q * P)
                    if q >= 2:
                        e.wait_ge(nc_c, 3 + l * 7 + q - 1)
                    pe.transpose(BM[q % 2][0:w, 0:P], flat[:, q * P:q * P + w], ident[:]).then_inc(nc_t, 1)

            ffn(0)
            mean_squares(NORMS["win"])
            e.wait_ge(h_lo, 3 * DC)
            ph = PH["win"]
            with e.Fori(0, ph.bodies) as i:
                for j in range(4):
                    if j % 2 == 0:
                        free(ph, i, j // 2)
                    tile(ph, i, j, 8, from_h(8 * (j % 2)), ph.bank(j // 2), j % 2 == 0, j % 2 == 1)

            e.wait_ge(nc_c, 10)
            e.wait_ge(a5v, 5)
            for k, r in enumerate((12, 13, 8, 9)):
                ins = pe.transpose(BM[0][:, k * PAIRS:(k + 1) * PAIRS], r5[:, r, :], ident[0:PAIRS, 0:PAIRS])
            ins.then_inc(t5, 1)
            for b in range(8):
                if b:
                    e.wait_ge(c5, b)
                if b == 4:
                    e.wait_ge(a5v, 6)
                src = (CX if b < 4 else BX)[:, b % 4 // 2]
                for k in range(4):
                    ins = pe.transpose(BM[(b + 1) % 2][:, k * P:(k + 1) * P], src[:, b % 2 * 4 + k, :], ident[:])
                ins.then_inc(t5, 1)
            e.wait_ge(c5, 8)
            e.wait_ge(in5, 16 * 9)
            for s in range(NS):
                ins = pe.transpose(BM[1][:, s * 64:(s + 1) * 64], io5[:, s, :], ident[0:64, 0:64])
            ins.then_inc(t5, 1)
            e.wait_ge(evac, PH["glu"].group(0, 0) + BANK_CREDIT)
            e.wait_ge(c5, 10)
            for k in range(PAIRS):
                j, q = k // 4, k % 4
                for r in range(2):
                    if k >= 2:
                        e.wait_ge((x5a, x5v)[r], k - 1)
                    pe.matmul((BA if k % 2 == 0 else BM)[r][:, 0:T], BTm[32 * q:32 * q + 32, j, r, :],
                              U5[32 * q:32 * q + 32, j, :], start=True, stop=True).then_inc(x5, 1)
            e.wait_ge(scan5, 1)
            for s in range(9):
                t = TP - 1 if s == 0 else TP + LS * s - 1
                if s >= 2:
                    e.wait_ge(fs_c, s - 1)
                pe.transpose(BM[s % 2][0:2 * PAIRS, 0:P], xs[:, :, :, t].rearrange("p r q -> p (r q)"), ident[:]).then_inc(fs_t, 1)
            for c in range(8):
                if c >= 2:
                    e.wait_ge(y5v, c - 1)
                for q in range(4):
                    for r in range(2):
                        ins = pe.matmul(BA[c % 2][32 * q:32 * q + 32, 0:T], CTm[:, c, r, 32 * q:32 * q + 32],
                                        xs[:, r, 4 * c + q, :], start=r == 0, stop=r == 1)
                ins.then_inc(y5, 1)
            e.wait_ge(act_lo, 16 + FFC + 8)
            ph = PH["glu"]
            with e.Fori(0, ph.bodies) as i:
                for j in range(4):
                    free(ph, i, j)
                    tile(ph, i, j, 8, from_act(0), j, True, True)
            ffn(1)
            mean_squares(NORMS["final"])
            for c in range(DC):
                e.wait_ge(yg_done, c + 1)
                if c >= 2:
                    e.wait_ge(y_c, c - 1)
                for t, (t0, n) in enumerate(((META, P), (META + P, P), (TP, NS * LS))):
                    ins = pe.transpose(bank[c % 2][0:n, t * P:(t + 1) * P], yg[:, c % 2, t0:t0 + n], ident[:])
                ins.then_inc(y_t, 1)


_INS = ["x_prompt", "x_sample", "state_a_conv", "state_a_h", "state_b_S", "state_c_re", "state_c_im", "state_ffn_conv",
        "meta_tokens", "g_mix", "w_in_e", "conv_a_w", "conv_a_b", "w_ra", "b_ra", "w_ia", "b_ia", "lam_a", "lb_logits",
        "gn_b", "w_out_e", "w_in_c", "lam_re", "lam_im", "log_dt", "bmat_re", "bmat_im", "cmat_re", "cmat_im", "d_skip",
        "w_glu_v", "w_glu_g", "g_ffn", "w_up", "w_gate", "conv_f_w", "conv_f_b", "w_down", "g_final"]
_OUTS = [("y_prompt", (1, SEQ, D)), ("y_sample", (NS, LS, D))] + [
    (f"{w}_{n}", shape(b)) for w, b in (("p", 1), ("s", NS)) for n, shape in (
        ("a_conv", lambda b: (1, b, 3, DA)), ("a_h", lambda b: (1, b, DA)), ("b_S", lambda b: (1, b, HEADS, P, P)),
        ("c_re", lambda b: (1, b, G5, P5)), ("c_im", lambda b: (1, b, G5, P5)), ("f_conv", lambda b: (2, b, 2, DFF)))]


def kernel(**inputs):
    import concourse.bacc as bacc
    from concourse.bass_utils import run_bass_kernel_spmd

    nc = bacc.Bacc("TRN2", target_bir_lowering=False, num_devices=1)
    rows = np.arange(P)
    odd = (rows // C5 % 2).astype(np.float32)
    arrays = {"c_ident": np.eye(P, dtype=np.float32),
              "c_masks": np.stack([1 - odd, odd, odd - 1, -odd], axis=1).astype(np.float32)}
    for name in _INS:
        arrays[name] = np.ascontiguousarray(inputs[name])
    a = {n: nc.dram_tensor(f"in_{n}", x.shape, mybir.dt.from_np(x.dtype), kind="ExternalInput").ap() for n, x in arrays.items()}
    o = {n: nc.dram_tensor(f"out_{n}", shape, F32, kind="ExternalOutput").ap() for n, shape in _OUTS}
    build(nc, a, o)
    r = run_bass_kernel_spmd(nc, [{f"in_{n}": x for n, x in arrays.items()}], core_ids=[0])
    return tuple(r.results[0][f"out_{n}"] for n, _ in _OUTS)
```

```python
import numpy as np
import concourse.bass as bass
from concourse import mybir
from contextlib import ExitStack

F32 = mybir.dt.float32
F32R = mybir.dt.float32r
ALU = mybir.AluOpType
ACT = mybir.ActivationFunctionType
ds = bass.ds

P = 128
D = 2048
DC = D // P
META, SEQ = 16, 256
TP = META + SEQ
NS, LS = 8, 8
T = TP + NS * LS
DA = D // 2
HEADS = DA // P
FFC = 43
DFF = FFC * P
EPS = 1e-6
C_RG = 8.0
RING = 4
TILE_K = 8
TW = TILE_K * P
PARTS = [(0, 15), (15, 14), (29, 14)]
G5, C5, P5 = 64, 16, 64
PAIRS = G5 // 2
CH = 16
POOL_PAIRS = 12
MID_PAIR = 22
DEAD = META - 2
NCH = T // CH
PCH = TP // CH
UNITS = PCH + NS
POOL_HEAD, DVE_HEAD, ROW_TURNS = 16, 33, 6
BANDS = {7: (0, 1, 2), 8: (3, 4, 5), 9: (6, 7, 8), 10: (9, 10, 11), 11: (12, 13, 14, 15)}
CREDIT = 4
BANK_CREDIT = 3

COL = {}
_n = 0
for _name, _w in (("g_mix", 32), ("g_ffn", 32), ("g_final", 16),
                  ("conv_f_w", 258), ("conv_f_b", 86),
                  ("conv_a_w", 32), ("conv_a_b", 8), ("b_ra", 8), ("b_ia", 8), ("lam_a", 8), ("lb", 8),
                  ("gn_b", 8), ("d_skip", 8), ("a_h", 64), ("a_conv", 192)):
    COL[_name] = _n
    _n += _w
PCOLS = _n


class Steps:

    def __init__(self, eng, sem):
        self.eng, self.sem, self.base, self.k, self.i, self.per = eng, sem, 0, 0, None, 0

    def then(self, ins):
        ins.then_inc(self.sem, 1)
        self.k += 1
        if self.i is None:
            self.eng.wait_ge(self.sem, self.base + self.k)
        else:
            self.eng.wait_ge(self.sem, self.i * self.per + (self.base + self.k))

    def mark(self, ins):
        ins.then_inc(self.sem, 1)
        self.k += 1
        return self.k

    def need(self, k):
        if self.i is None:
            self.eng.wait_ge(self.sem, self.base + k)
        else:
            self.eng.wait_ge(self.sem, self.i * self.per + (self.base + k))

    def enter(self, i, per, first=0):
        self.base += self.k - first * per
        self.k, self.i, self.per = 0, i, per

    def leave(self, end):
        assert self.k == self.per, (self.k, self.per)
        self.base += end * self.per
        self.k, self.i = 0, None


class Phase:
    def __init__(self, name, bodies, tiles, groups, banks, tile0, group0):
        self.name, self.bodies, self.tiles, self.groups, self.banks = name, bodies, tiles, groups, banks
        self.tile0, self.group0 = tile0, group0

    def tile(self, i, j):
        return i * self.tiles + (self.tile0 + j)

    def slot_use(self, i, j):
        return i * (self.tiles // RING) + ((self.tile0 + j) // RING + 1)

    def group(self, i, r):
        return i * self.groups + (self.group0 + r)

    def bank(self, r):
        return r % self.banks


def plan():
    out, t, g = {}, 0, 0
    rows = [("head", HEADS, 12, 6, 3), ("wout", 8, 4, 2, 2)]
    ffn = lambda l: [x for p, (_, n) in enumerate(PARTS)
                     for x in ((f"up{l}{p}", n, 4, 2, 2), (f"down{l}{p}", 8, 4, 2, 2))]
    rows += ffn(0) + [("win", 4, 4, 2, 2), ("glu", 8, 4, 4, 4)] + ffn(1)
    for name, b, ti, gr, banks in rows:
        out[name] = Phase(name, b, ti, gr, banks, t, g)
        t += b * ti
        g += b * gr
    return out, t


def halves(n):
    return [(0, (n + 1) // 2), ((n + 1) // 2, n // 2)]


def conv_row_parts(total, own):
    out = []
    for q in range(-(-total // P)):
        a, b = q * P, min(total, (q + 1) * P)
        if a < own:
            out.append((q, 0, min(b, own) - a, "p", a))
        if b > own:
            lo = max(a, own)
            out.append((q, lo - a, b - lo, "s", lo - own))
    return out


STORES_A = len(conv_row_parts(216, 24)) + 2
STORES_F = len(conv_row_parts(774, 86))
STORES_C = 4


def build(nc, a, o):
    PH, _ = plan()
    ctx = ExitStack()
    with ctx:
        def sb(name, shape, dt=F32):
            return ctx.enter_context(nc.sbuf_tensor(name, shape, dt))

        def sem(name):
            return ctx.enter_context(nc.semaphore(name))

        X = sb("X", [P, DC, T])
        raw = sb("raw", [P, RING, TW])
        wh = sb("wh", [P, RING, TW], F32R)
        wl = sb("wl", [P, RING, TW], F32R)
        prm = sb("prm", [P, PCOLS])
        ident = sb("ident", [P, P])
        ones = sb("ones", [P, P])
        masks = sb("masks", [P, 4])
        rs = sb("rs", [P, T])
        ssq = sb("ssq", [P, T])
        sq = sb("sq", [P, T])
        hlast = sb("hlast", [P, 1 + NS, HEADS])
        ncva = sb("ncva", [P, 1 + NS, 3, HEADS])
        tiny = sb("tiny", [P, 12, HEADS])
        rate, lbm, oml = tiny[:, 0, :], tiny[:, 1, :], tiny[:, 2, :]
        arena = nc.sbuf_base
        arena += -arena % 32

        def place(name, shape, at, dt=F32):
            t = nc.alloc_sbuf_tensor_at(name, shape, dt, offset=arena + at)
            size = 4 * int(np.prod(shape[1:]))
            assert arena + at + size <= nc.sbuf_usable_end, (name, arena + at + size - nc.sbuf_usable_end)
            return t, at + size + (-size % 32)

        act, at_h = place("act", [P, 16, 2, T], 0, F32R)
        h, at_u = place("h", [P, DC, 2, T], at_h, F32R)

        def union(at, *items):
            out = []
            for name, shape in items:
                t, at = place(name, shape, at)
                out.append(t)
            return out

        xin, rows = union(at_u, ("xin", [P, 3, D]), ("rows", [P, 9, P]))
        (XA, CT, IG, AA, HH, GA, Q, FZ, V, GB, SB, K, FM, D1, EN, QF, PB, W, OB, KM, KM3, TK, TV, WR, SS, SR, FE) = union(
            at_u, ("XA", [P, 363]), ("CT", [P, 363]), ("IG", [P, T]), ("AA", [P, T]), ("HH", [P, T]), ("GA", [P, T]),
            ("Q", [P, T]), ("FZ", [P, T]), ("V", [P, T]), ("GB", [P, T]), ("SB", [P, T]), ("K", [P, T]),
            ("FM", [P, T + 1]), ("D1", [P, T]), ("EN", [P, T]), ("QF", [P, T]), ("PB", [P, 2, T]), ("W", [P, T]),
            ("OB", [P, T]), ("KM", [P, 2, 256]), ("KM3", [P, 4, 96]), ("TK", [P, 8, P]), ("TV", [P, 3, P]),
            ("WR", [P, 2, P]), ("SS", [P, NS, P]), ("SR", [P, 8, P]), ("FE", [P, UNITS]))
        slot_bytes = 2 * T * 4
        XC, RT = union(14 * slot_bytes, ("XC", [P, T]), ("RT", [P, T]))
        GG, = union(15 * slot_bytes, ("GG", [P, 2, T]))
        UPW = 2 + TP + NS * (2 + LS)
        UP, CV, GT, AC, SF, NCF, srow, orow = union(
            at_u, ("UP", [P, UPW]), ("CV", [P, UPW]), ("GT", [P, T]), ("AC", [P, T]),
            ("SF", [P, NS * 2, FFC]), ("NCF", [P, 1 + NS, 2, FFC]), ("srow", [P, 6, P]), ("orow", [P, 7, P]))
        xs, _ = place("xs", [P, 2, PAIRS, T], 0)
        U5, CTm, BTm, A5, st5, ys5, tmp5, car5, A16 = union(
            at_u, ("U5", [P, 8, T]), ("CTm", [P, 8, 2, P]), ("BTm", [P, 8, 2, P]), ("A5", [P, 2, 2, PAIRS]),
            ("st5", [P, NS, 2, PAIRS]), ("ys5", [P, 2, T]), ("tmp5", [P, 2, 2 * PAIRS * (TP // CH)]), ("car5", [P, 2, PAIRS, TP // CH - 1]), ("A16", [P, 2, 2, PAIRS]))
        fin5, = union(at_u + 4 * (8 * T + 32 * P + 4 * PAIRS + NS * 2 * PAIRS + 2 * T), ("fin5", [P, 1 + NS, 2, PAIRS]))
        io5o, = union(at_u + 4 * (8 * T + 16 * P), ("io5o", [2 * PAIRS, 9, P]))
        r5, CN, CX, Bn, BX, B2, io5, zz = union(
            0, ("r5", [PAIRS, 16, P]), ("CN", [P, 2, 8, P5]), ("CX", [P, 2, 8, P]), ("Bn", [P, 2, PAIRS, C5]),
            ("BX", [P, 2, 8, P]), ("B2", [P, 2, PAIRS, C5]), ("io5", [2 * PAIRS, NS, P]), ("zz", [P, 4, PAIRS]))
        GS, VT = union(at_u, ("GS", [P, T]), ("VT", [P, T]))
        yg, yo = union(at_u, ("yg", [P, 2, T]), ("yo", [P, 3, D]))

        bank = [ctx.enter_context(nc.psum_tensor(f"bank{i}", [P, 512], F32)) for i in range(8)]
        BA = (bank[3], bank[4])
        BM = (bank[5], bank[6])
        BO = bank[7]
        YORDER = (0, 1, 2, 3, 4, 5, 6, 7)
        YBANK = (0, 1, 2, 3, 4, 7, 0, 1)

        landed = [sem(f"landed{s}") for s in range(RING)]
        rounded = sem("rounded")
        split = sem("split")
        used = sem("used")
        evac = sem("evac")
        h_hi, h_lo = sem("h_hi"), sem("h_lo")
        act_hi, act_lo = sem("act_hi"), sem("act_lo")
        ssq_added = sem("ssq_added")
        ms_done = sem("ms_done")
        ms_inv = sem("ms_inv")
        rstd = sem("rstd")
        dchain, pchain = sem("dchain"), sem("pchain")
        consts_in, rows_in, x_in = sem("consts_in"), sem("rows_in"), sem("x_in")
        rows_t, rows_c = sem("rows_t"), sem("rows_c")
        x_t, x_c = sem("x_t"), sem("x_c")
        once = sem("once")
        lam_v, lam_a = sem("lam_v"), sem("lam_a")
        out_dma = sem("out_dma")
        sg, sk, bandin, sfx, km = sem("sg"), sem("sk"), sem("bandin"), sem("sfx"), sem("km")
        p_ready, a_ready, a_used = sem("p_ready"), sem("a_ready"), sem("a_used")
        conv_in, ct, xc, gates, gates_read = sem("conv_in"), sem("ct"), sem("xc"), sem("gates"), sem("gates_read")
        aa, th, t_in, mu, b_ready, ga, oa = sem("aa"), sem("th"), sem("t_in"), sem("mu"), sem("b_ready"), sem("ga"), sem("oa")
        kt, tk_copied = sem("kt"), sem("tk_copied")
        row_turn = sem("row_turn")
        u_ready, s_done, inter = sem("u_ready"), sem("s_done"), sem("inter")
        sbg, oo, oms, oinv, osq, ob = sem("sbg"), sem("oo"), sem("oms"), sem("oinv"), sem("osq"), sem("ob")
        wr_in, ss_in, s_out = sem("wr_in"), sem("ss_in"), sem("s_out")
        up_in, cv0, cv2, gelu, prod = sem("up_in"), sem("cv0"), sem("cv2"), sem("gelu"), sem("prod")
        sf_in, sf_t, sf_c = sem("sf_in"), sem("sf_t"), sem("sf_c")
        nc_t, nc_c, nc_v = sem("nc_t"), sem("nc_c"), sem("nc_v")
        in5, a5v, a5a, t5, c5, x5, x5a = (sem(n) for n in ("in5", "a5v", "a5a", "t5", "c5", "x5", "x5a"))
        scan5, scan5p, a16, fs_t, fs_c, y5, y5v, y5g = (sem(n) for n in ("scan5", "scan5p", "a16", "fs_t", "fs_c", "y5", "y5v", "y5g"))
        gsig = sem("gsig")
        yg_done, y_t, y_c = sem("yg_done"), sem("y_t"), sem("y_c")

        block = ctx.enter_context(nc.Block())

        def one(t, c):
            return t[:, ds(c, 1), :].rearrange("p a t -> p (a t)")

        def part(t, c, r):
            return t[:, ds(c, 1), r, :].rearrange("p a t -> p (a t)")

        def col(name, k=0):
            return prm[:, COL[name] + k:COL[name] + k + 1]

        def dcol(name, i, k=0):
            return prm[:, ds(i + (COL[name] + k), 1)]

        def padded(t, start, pitch):
            return t[:, start:start + NS * pitch].rearrange("p (s w) -> p s w", w=pitch)

        def samples(t):
            return t[:, TP:T].rearrange("p (s w) -> p s w", w=LS)

        def bands(t, d):
            return t[:, 0:T].rearrange("p (c w) -> p c w", w=CH)[:, :, d:CH]

        XAs, CTs = padded(XA, 3 + TP, 3 + LS), padded(CT, 3 + TP, 3 + LS)
        UPs, CVs = padded(UP, 2 + TP, 2 + LS), padded(CV, 2 + TP, 2 + LS)
        NORMS = {"head": 0, "up00": 1, "win": 2, "up10": 3, "final": 4}

        def scan_pairs(eng, st, groups):
            n = TP // CH

            def step(coef, prev, cur, cols, add_to=None):
                def A(k, g):
                    c = coef[:, k, :, g[0]:g[1]]
                    return c if cols == 1 else c.unsqueeze(3).to_broadcast([P, 2, g[1] - g[0], cols])

                def m(k, g):
                    nq = g[1] - g[0]
                    t = tmp5[:, k, 2 * n * g[0]:2 * n * g[0] + 2 * nq * cols]
                    return t.rearrange("p (r q) -> p r q", r=2) if cols == 1 else t.rearrange("p (r q c) -> p r q c", r=2, q=nq)

                start, products, sums = st.k, [], []
                for x, g in enumerate(groups):
                    st.need(start - (len(groups) - 1 - x))
                    p = prev(g)
                    eng.tensor_tensor(m(0, g), A(0, g), p, ALU.mult)
                    eng.tensor_tensor(m(1, g)[:, 0], A(1, g)[:, 0], p[:, 1], ALU.mult)
                    products.append(st.mark(eng.tensor_tensor(m(1, g)[:, 1], A(1, g)[:, 1], p[:, 0], ALU.mult)))
                for x, g in enumerate(groups):
                    st.need(products[x])
                    to = m(0, g) if add_to is None else cur(g)
                    sums.append(st.mark(eng.tensor_tensor(to, m(0, g), m(1, g), ALU.add)))
                for x, g in enumerate(groups):
                    st.need(sums[x])
                    to, more = (cur(g), m(0, g)) if add_to is None else (add_to(g), cur(g))
                    st.mark(eng.tensor_tensor(to, to, more, ALU.add))

            per = 3 * len(groups)
            xp = lambda g: xs[:, :, g[0]:g[1], 0:TP].rearrange("p r q (c w) -> p r q c w", w=CH)
            xsm = lambda g: xs[:, :, g[0]:g[1], TP:T].rearrange("p r q (s w) -> p r q s w", w=LS)
            at = lambda v, w: v[:, :, :, :, ds(w, 1)].rearrange("p r q c a -> p r q (c a)")
            step(A5, lambda g: st5.rearrange("p s r q -> p r q s")[:, :, g[0]:g[1]], lambda g: xsm(g)[:, :, :, :, 0], NS)
            with st.eng.Fori(0, LS - 1) as i:
                st.enter(i, per)
                step(A5, lambda g: at(xsm(g), i), lambda g: at(xsm(g), i + 1), NS)
                st.leave(LS - 1)
            with st.eng.Fori(0, CH - 1) as i:
                st.enter(i, per)
                step(A5, lambda g: at(xp(g), i), lambda g: at(xp(g), i + 1), n)
                st.leave(CH - 1)
            last = lambda g, c: xs[:, :, g[0]:g[1], ds(c * CH + (CH - 1), 1)].rearrange("p r q a -> p r (q a)")
            with st.eng.Fori(0, n - 1) as i:
                st.enter(i, per)
                step(A16, lambda g: last(g, i), lambda g: last(g, i + 1), 1)
                st.leave(n - 1)
            car = lambda g: car5[:, :, g[0]:g[1]]
            step(A5, lambda g: xp(g)[:, :, :, 0:n - 1, CH - 1], car, n - 1, lambda g: xp(g)[:, :, :, 1:n, 0])
            with st.eng.Fori(0, CH - 2) as i:
                st.enter(i, per)
                step(A5, car, car, n - 1, lambda g: at(xp(g), i + 1)[:, :, :, 1:n])
                st.leave(CH - 2)
            st.need(st.k)

        @block.sync
        def _(e):
            flat = lambda x: x.rearrange("(c p) -> c p", p=P)
            rowsets = [
                [(a["g_mix"].rearrange("l (c p) -> (l c) p", p=P), 32), (a["g_ffn"].rearrange("l (c p) -> (l c) p", p=P), 32),
                 (flat(a["g_final"]), 16)],
                *[[(a["conv_f_w"].rearrange("l k (c p) -> (l k c) p", p=P)[86 * q:86 * q + 86], 86)] for q in range(3)],
                [(a["conv_f_b"].rearrange("l (c p) -> (l c) p", p=P), 86)],
                [(a["conv_a_w"][0].rearrange("k (c p) -> (k c) p", p=P), 32), (flat(a["conv_a_b"][0]), 8),
                 (a["b_ra"][0], 8), (a["b_ia"][0], 8), (flat(a["lam_a"][0]), 8), (flat(a["lb_logits"][0]), 8),
                 (flat(a["gn_b"][0]), 8), (flat(a["d_skip"][0]), 8)],
                [(a["state_a_h"][0].rearrange("s (c p) -> (s c) p", p=P), 64)],
                *[[(a["state_a_conv"][0].rearrange("s r (c p) -> (s r c) p", p=P)[96 * q:96 * q + 96], 96)] for q in range(2)],
            ]
            e.dma_start(ident[:], a["c_ident"]).then_inc(consts_in, 16)
            e.dma_start(masks[:], a["c_masks"]).then_inc(consts_in, 16)
            xp, xsm = a["x_prompt"][0], a["x_sample"].rearrange("s t d -> (s t) d")
            for dst, src in ((xin[0:META, 0, :], a["meta_tokens"]), (xin[META:P, 0, :], xp[0:P - META]),
                             (xin[:, 1, :], xp[P - META:2 * P - META]), (xin[0:META, 2, :], xp[2 * P - META:SEQ]),
                             (xin[META:META + NS * LS, 2, :], xsm)):
                e.dma_start(dst, src).then_inc(x_in, 16)
            for q, sets in enumerate(rowsets):
                r = 0
                for src, n in sets:
                    e.dma_start(rows[r:r + n, q, :], src).then_inc(rows_in, 16)
                    r += n

            def load(ph, i, j, w, k0, kn, c):
                e.wait_ge(split, ph.tile(i, j) + 1)
                e.dma_start(raw[:, j % RING, 0:kn * P].rearrange("p (k n) -> p k n", k=kn),
                            w[k0 * P:(k0 + kn) * P, ds(c, P)].rearrange("(k p) n -> p k n", p=P)) \
                    .then_inc(landed[j % RING], 16)

            ph = PH["head"]
            columns = [2 * DA, 3 * DA, 4 * DA, 0, 5 * DA, DA]
            with e.Fori(0, HEADS) as i:
                for j in range(12):
                    load(ph, i, j, a["w_in_e"][0], 8 * (j % 2), 8, (i + 1) * P + (columns[j // 2] - P))
            with e.Fori(0, 8) as i:
                for j in range(4):
                    load(PH["wout"], i, j, a["w_out_e"][0], 8 * (j % 2), 8, i * (2 * P) + (j // 2) * P)

            def ffn(l):
                for p, (f0, n) in enumerate(PARTS):
                    with e.Fori(0, n) as i:
                        for j in range(4):
                            load(PH[f"up{l}{p}"], i, j, a["w_up" if j < 2 else "w_gate"][l], 8 * (j % 2), 8, i * P + f0 * P)
                    with e.Fori(0, 8) as i:
                        for j in range(4):
                            k0, kn = halves(n)[j % 2]
                            load(PH[f"down{l}{p}"], i, j, a["w_down"][l], f0 + k0, kn, i * (2 * P) + (j // 2) * P)

            ffn(0)
            with e.Fori(0, 4) as i:
                for j in range(4):
                    load(PH["win"], i, j, a["w_in_c"][0], 8 * (j % 2), 8, i * (2 * P) + (j // 2) * P)
            with e.Fori(0, 8) as i:
                for j in range(4):
                    load(PH["glu"], i, j, a["w_glu_v" if j % 2 == 0 else "w_glu_g"][0], 0, 8, i * (2 * P) + (j // 2) * P)
            ffn(1)

        @block.scalar
        def _(e):
            sc = nc.scalar

            def round_tile(ph, i, j):
                e.wait_ge(landed[j % RING], (ph.slot_use(i, j) + 1) * 16)
                e.wait_ge(used, ph.tile(i, j) + 1 + RING)
                sc.activation(wh[:, j % RING, :], raw[:, j % RING, :], ACT.Copy).then_inc(rounded, 1)

            def hi_of_x(ph, i, r, g, c):
                e.wait_ge(evac, ph.group(i, r) + 1 + BANK_CREDIT)
                sc.activation(part(h, c, 0), one(X, c), ACT.Copy, scale=prm[:, ds(c + g, 1)]).then_inc(h_hi, 1)

            def norm_root(n):
                e.wait_ge(ms_inv, n + 1)
                sc.activation(rs[:], rs[:], ACT.Sqrt).then_inc(rstd, 1)

            for q in range(9):
                w = (80, 86, 86, 86, 86, 88, 64, 96, 96)[q]
                c0 = (0, 80, 166, 252, 338, 424, 512, 576, 672)[q]
                e.wait_ge(rows_t, q + 1)
                sc.activation(prm[:, c0:c0 + w], BM[q % 2][:, 0:w], ACT.Copy).then_inc(rows_c, 1)
            e.wait_ge(rows_c, 9)
            for c in range(DC):
                e.wait_ge(x_c, c + 1)
                sc.activation(h[:, c, 0, :], X[:, c, :], ACT.Copy, scale=col("g_mix", c)).then_inc(h_hi, 1)
            e.wait_ge(lam_v, 1)
            sc.activation(tiny[:, 4, :], tiny[:, 3, :], ACT.Exp, scale=-1.0)
            sc.activation(tiny[:, 6, :], tiny[:, 5, :], ACT.Exp).then_inc(lam_a, 1)
            for j in range(RING):
                e.wait_ge(landed[j], 16)
                e.wait_ge(used, j + 1)
                sc.activation(wh[:, j, :], raw[:, j, :], ACT.Copy).then_inc(rounded, 1)
            norm_root(0)

            ph = PH["head"]

            def head(i, ended):
                n = i + 1
                for j in range(12):
                    round_tile(ph, i, j)
                    if ended:
                        end_of(i - 1, j)
                    if j == 3:
                        e.wait_ge(evac, ph.group(i, 1) + 1 + BANK_CREDIT)
                        sc.activation(FM[:, 0:T], FZ[:], ACT.Sigmoid).then_inc(sg, 1)
                        sc.activation(K[:], FZ[:], ACT.Sigmoid, scale=-1.0).then_inc(sk, 1)
                    if j == 7:
                        e.wait_ge(conv_in, n)
                        sc.activation(CT[:, 0:360], XA[:, 3:363], ACT.Identity, scale=dcol("conv_a_w", i, 24),
                                      bias=dcol("conv_a_b", i)).then_inc(ct, 1)
                    if j == 9:
                        e.wait_ge(kt, i * 3 + 1)
                        sc.activation(TK[:, 0:4, :], BM[0][:].rearrange("p (a n) -> p a n", a=4), ACT.Copy).then_inc(tk_copied, 1)
                        e.wait_ge(kt, i * 3 + 2)
                        sc.activation(TK[0:80, 4:8, :], BM[1][0:80, :].rearrange("p (a n) -> p a n", a=4), ACT.Copy) \
                            .then_inc(tk_copied, 1)
                        e.wait_ge(kt, i * 3 + 3)
                        sc.activation(TV[:, 0:2, :], BO[:, 0:256].rearrange("p (a n) -> p a n", a=2), ACT.Copy)
                        sc.activation(TV[0:80, 2, :], BO[0:80, 256:384], ACT.Copy).then_inc(tk_copied, 1)
                        e.wait_ge(evac, ph.group(i, 4) + 1 + BANK_CREDIT)
                        sc.activation(SB[:], GB[:], ACT.Sigmoid).then_inc(sbg, 1)
                    if j == 10:
                        e.wait_ge(gates, n)
                        sc.activation(RT[:], BM[0][:, 0:T], ACT.Sigmoid, bias=dcol("b_ra", i))
                        sc.activation(IG[:], BM[1][:, 0:T], ACT.Sigmoid, bias=dcol("b_ia", i)).then_inc(gates_read, 1)
                        e.wait_ge(gates_read, n)
                        sc.activation(AA[:], RT[:], ACT.Exp, scale=tiny[:, 0, ds(i, 1)]).then_inc(aa, 1)
                        sc.activation(CT[:, 0:T], RT[:], ACT.Tanh, scale=tiny[:, 0, ds(i, 1)]).then_inc(th, 1)
                    if j == 11:
                        e.wait_ge(t_in, n)
                        sc.activation(RT[:], RT[:], ACT.Sqrt, scale=-1.0).then_inc(mu, 1)

            def end_of(i, j):
                n = i + 1
                if j == 0:
                    e.wait_ge(evac, ph.group(i, 5) + 1 + BANK_CREDIT)
                    sc.activation(GA[:], GA[:], ACT.Gelu_apprx_tanh).then_inc(ga, 1)
                if j == 2:
                    e.wait_ge(oa, n)
                    sc.activation(part(act, i * 2, 0), HH[:], ACT.Copy).then_inc(act_hi, 1)
                if j == 5:
                    e.wait_ge(s_done, n * (UNITS + 1))
                    e.dma_start(o["p_b_S"][0, 0, ds(i, 1)].rearrange("a k v -> k (a v)"), SR[:, PCH % 8, :]).then_inc(s_out, 16)
                    e.dma_start(o["s_b_S"][0, :, ds(i, 1)].rearrange("s a k v -> k s (a v)"), SS[:]).then_inc(s_out, 16)
                    e.wait_ge(oinv, n)
                    sc.activation(SB[:], SB[:], ACT.Sqrt).then_inc(osq, 1)
                if j == 6:
                    e.wait_ge(ob, n)
                    sc.activation(part(act, i * 2 + 1, 0), OB[:], ACT.Copy).then_inc(act_hi, 1)

            head(0, False)
            with e.Fori(1, HEADS) as i:
                head(i, True)
            for j in range(7):
                end_of(HEADS - 1, j)

            ph = PH["wout"]
            with e.Fori(0, ph.bodies) as i:
                for j in range(4):
                    round_tile(ph, i, j)
                    if j % 2:
                        hi_of_x(ph, i, j // 2, COL["g_ffn"], i * 2 + j // 2)

            def store_rows(src, parts, dst_p, dst_s):
                for q, r0, n, whose, to in parts:
                    dst = dst_p if whose == "p" else dst_s
                    e.dma_start(dst[to:to + n], src[r0:r0 + n, q, :]).then_inc(out_dma, 16)

            for q in range(3):
                w = (P, 216 - P, 72)[q]
                e.wait_ge(nc_t, q + 1)
                sc.activation(orow[0:w, q, :], BM[q % 2][0:w, 0:P], ACT.Copy).then_inc(nc_c, 1)
            e.wait_ge(nc_c, 3)
            store_rows(orow, conv_row_parts(216, 24), o["p_a_conv"][0].rearrange("s r (c p) -> (s r c) p", p=P),
                       o["s_a_conv"][0].rearrange("s r (c p) -> (s r c) p", p=P))
            e.dma_start(o["p_a_h"][0].rearrange("s (c p) -> (s c) p", p=P), orow[0:8, 2, :]).then_inc(out_dma, 16)
            e.dma_start(o["s_a_h"][0].rearrange("s (c p) -> (s c) p", p=P), orow[8:72, 2, :]).then_inc(out_dma, 16)

            def ffn(l, gnext):
                for q in range(6):
                    w = min(P, 688 - q * P)
                    e.wait_ge(sf_t, l * 6 + q + 1)
                    sc.activation(SF.rearrange("p a f -> p (a f)")[:, q * P:q * P + w], BM[q % 2][:, 0:w], ACT.Copy).then_inc(sf_c, 1)
                norm_root(NORMS[f"up{l}0"])
                for p, (f0, n) in enumerate(PARTS):
                    ph = PH[f"up{l}{p}"]
                    cc = l * FFC + f0
                    with e.Fori(0, n) as i:
                        for j in range(4):
                            round_tile(ph, i, j)
                            if j == 1:
                                e.wait_ge(up_in, i + (cc + 1))
                                sc.activation(CV[:, 0:UPW - 2], UP[:, 2:UPW], ACT.Identity,
                                              scale=dcol("conv_f_w", i, (l * 3 + 2) * FFC + f0),
                                              bias=dcol("conv_f_b", i, l * FFC + f0)).then_inc(cv0, 1)
                            if j == 2:
                                e.wait_ge(cv2, i + (cc + 1))
                                sc.activation(CV[:, 0:UPW - 2], CV[:, 0:UPW - 2], ACT.Gelu_apprx_tanh).then_inc(gelu, 1)
                            if j == 3:
                                e.wait_ge(prod, i + (cc + 1))
                                sc.activation(part(act, i, 0), AC[:], ACT.Copy).then_inc(act_hi, 1)
                    ph = PH[f"down{l}{p}"]
                    last = p == len(PARTS) - 1
                    with e.Fori(0, ph.bodies - (last and l == 1)) as i:
                        for j in range(4):
                            round_tile(ph, i, j)
                            if last and gnext is not None and j % 2:
                                hi_of_x(ph, i, j // 2, gnext, i * 2 + j // 2)
                e.wait_ge(out_dma, 16 * (STORES_A if l == 0 else STORES_A + STORES_F + STORES_C))
                for q in range(7):
                    w = min(P, 774 - q * P)
                    e.wait_ge(nc_t, 3 + l * 7 + q + 1)
                    sc.activation(orow[0:w, q, :], BM[q % 2][0:w, 0:P], ACT.Copy).then_inc(nc_c, 1)
                e.wait_ge(nc_c, 3 + l * 7 + 7)
                store_rows(orow, conv_row_parts(774, 86), o["p_f_conv"][l].rearrange("s r (c p) -> (s r c) p", p=P),
                           o["s_f_conv"][l].rearrange("s r (c p) -> (s r c) p", p=P))

            ffn(0, COL["g_mix"] + DC)
            norm_root(NORMS["win"])
            ph = PH["win"]
            with e.Fori(0, 2) as i:
                for j in range(4):
                    round_tile(ph, i, j)
            e.wait_ge(a5v, 1)
            sc.activation(r5[:, 3, 0:2], r5[:, 2, 0:2], ACT.Exp).then_inc(a5a, 1)
            e.wait_ge(a5v, 2)
            sc.activation(r5[:, 6, :], r5[:, 5, :], ACT.Exp).then_inc(a5a, 1)
            e.wait_ge(a5v, 3)
            sc.activation(r5[:, 10, :], r5[:, 9, :], ACT.Sin)
            sc.activation(r5[:, 11, :], r5[:, 9, :], ACT.Sin, scale=0.5).then_inc(a5a, 1)
            with e.Fori(2, ph.bodies) as i:
                for j in range(4):
                    round_tile(ph, i, j)
            for k in range(PAIRS):
                for r in range(2):
                    e.wait_ge(x5, 2 * k + r + 1)
                    sc.activation(xs[:, r, k, :], (BA if k % 2 == 0 else BM)[r][:, 0:T], ACT.Copy).then_inc(x5a, 1)
            for k, c in enumerate(YORDER):
                e.wait_ge(y5v, k + 1)
                sc.activation(ys5[:, k % 2], ys5[:, k % 2], ACT.Gelu_apprx_tanh).then_inc(y5g, 1)
                e.wait_ge(y5g, k + 1)
                if k == 0:
                    e.wait_ge(y5, 2)
                sc.activation(act[:, c, 0, :], ys5[:, k % 2], ACT.Copy).then_inc(act_hi, 1)
            for s in range(9):
                e.wait_ge(fs_t, s + 1)
                sc.activation(io5o[:, s, :], BM[s % 2][0:2 * PAIRS, 0:P], ACT.Copy).then_inc(fs_c, 1)
            e.wait_ge(fs_c, 9)
            for r, (np_, ns_) in enumerate((("p_c_re", "s_c_re"), ("p_c_im", "s_c_im"))):
                e.dma_start(o[np_][0, 0].rearrange("(q g) p -> q (g p)", g=2), io5o[32 * r:32 * r + 32, 0, :]).then_inc(out_dma, 16)
                e.dma_start(o[ns_][0].rearrange("s (q g) p -> q s (g p)", g=2), io5o[32 * r:32 * r + 32, 1:9, :]).then_inc(out_dma, 16)

            ph = PH["glu"]
            with e.Fori(0, ph.bodies) as i:
                for j in range(4):
                    round_tile(ph, i, j)
                    if j % 2:
                        e.wait_ge(used, ph.tile(i, j) + 1 + CREDIT)
                        sc.activation(GS[:], bank[j][:, 0:T], ACT.Sigmoid).then_inc(gsig, 1)
                        hi_of_x(ph, i, j, COL["g_ffn"] + DC, i * 2 + j // 2)
            ffn(1, None)
            norm_root(NORMS["final"])
            e.wait_ge(out_dma, 16 * (STORES_A + 2 * STORES_F + STORES_C))
            for c in range(DC):
                e.wait_ge(y_t, c + 1)
                sc.activation(yo[:, 0:2, c * P:(c + 1) * P], bank[c % 2][:, 0:256].rearrange("p (a n) -> p a n", a=2), ACT.Copy)
                sc.activation(yo[0:64, 2, c * P:(c + 1) * P], bank[c % 2][0:64, 256:384], ACT.Copy).then_inc(y_c, 1)
                if c % 4 == 3:
                    c0, c1 = (c - 3) * P, (c + 1) * P
                    e.wait_ge(y_c, c + 1)
                    e.dma_start(o["y_prompt"][0, 0:P, c0:c1], yo[:, 0, c0:c1]).then_inc(out_dma, 16)
                    e.dma_start(o["y_prompt"][0, P:2 * P, c0:c1], yo[:, 1, c0:c1]).then_inc(out_dma, 16)
                    e.dma_start(o["y_sample"].rearrange("s t d -> (s t) d")[:, c0:c1], yo[0:64, 2, c0:c1]).then_inc(out_dma, 16)
            e.wait_ge(out_dma, 16 * (STORES_A + 2 * STORES_F + STORES_C + 12))
            e.wait_ge(s_out, 32 * HEADS + 16)

        @block.gpsimd
        def _(e):
            gp = nc.gpsimd
            st = Steps(e, pchain)

            def square(xc, first):
                if first:
                    gp.tensor_tensor(ssq[:], xc, xc, ALU.mult).then_inc(ssq_added, 1)
                else:
                    st.then(gp.tensor_tensor(sq[:], xc, xc, ALU.mult))
                    gp.tensor_tensor(ssq[:], ssq[:], sq[:], ALU.add).then_inc(ssq_added, 1)

            for c in range(DC):
                e.wait_ge(x_c, c + 1)
                if c:
                    e.wait_ge(ssq_added, c)
                square(X[:, c, :], c == 0)
            e.wait_ge(once, 1)

            with e.Fori(0, HEADS) as i:
                n = i + 1
                e.dma_start(WR[:, 0, :], a["w_ra"][0, ds(i, 1)].rearrange("a k n -> k (a n)")).then_inc(wr_in, 16)
                e.dma_start(WR[:, 1, :], a["w_ia"][0, ds(i, 1)].rearrange("a k n -> k (a n)")).then_inc(wr_in, 16)
                st.enter(i, POOL_HEAD)
                e.wait_ge(bandin, n)
                for d in range(CH):
                    """G_d[t] = k[t-d] * f[t-d+1] ... f[t]; its product with q summed over k's features is the
                    attention of token t to token t-d."""
                    w = CH - d
                    if d == 10:
                        e.wait_ge(s_out, i * 32 + 16)
                    if d == 1:
                        st.then(gp.tensor_tensor(bands(GG[:, 1, :], 1), bands(FM, 1), bands(K, 0)[:, :, 0:CH - 1], ALU.mult))
                    elif d > 1:
                        st.then(gp.tensor_tensor(bands(GG[:, d % 2, :], d), bands(FM, d),
                                                 bands(GG[:, (d - 1) % 2, :], d - 1)[:, :, 0:w], ALU.mult))
                    e.wait_ge(a_ready, i * CH + (d + 1))
                    gp.tensor_tensor(PB[:, d % 2, 0:NCH * w].rearrange("p (c w) -> p c w", w=w), bands(Q, d),
                                     bands(K, 0) if d == 0 else bands(GG[:, d % 2, :], d), ALU.mult).then_inc(p_ready, 1)
                    if d == 10:
                        e.dma_start(SS[:], a["state_b_S"][0, :, ds(i, 1)].rearrange("s a k v -> k s (a v)")).then_inc(ss_in, 16)
                    if d == 1:
                        e.wait_ge(sfx, n)
                        for par in range(2):
                            v = lambda t: t.rearrange("p (c q w) -> p c q w", q=2, w=CH)[:, :, par, :]
                            gp.tensor_tensor(v(KM[:, par, :]), v(K[:, 0:256]), v(FZ[:, 0:256]), ALU.mult)
                        for m in range(4):
                            nb = 3 if m < 2 else 2
                            for b in range(nb):
                                c0 = 32 * b + 8 * m
                                ins = gp.tensor_tensor(KM3[:, m, c0:c0 + 8], K[:, 256 + c0:264 + c0], FZ[:, 256 + c0:264 + c0], ALU.mult)
                        ins.then_inc(km, 1)
                e.wait_ge(gates_read, n)
                st.then(gp.tensor_tensor(IG[:], IG[:], XC[:], ALU.mult))
                e.wait_ge(mu, n)
                gp.tensor_tensor(IG[:, 1:T], IG[:, 1:T], RT[:, 1:T], ALU.mult).then_inc(b_ready, 1)
                st.leave(HEADS)

            def squares(ph, groups, norm):
                e.wait_ge(ms_done, norm)
                st.then(gp.memset(ssq[:], 0.0))
                with e.Fori(0, ph.bodies) as i:
                    st.enter(i, 2)
                    for r in range(2):
                        e.wait_ge(evac, ph.group(i, groups[r]) + 1 + BANK_CREDIT)
                        e.wait_ge(ssq_added, i * 2 + (norm * DC + r))
                        square(one(X, i * 2 + r), False)
                    st.leave(ph.bodies)

            def load_past(l):
                src = a["state_ffn_conv"][l].rearrange("s r (c p) -> (s r c) p", p=P)
                for q in range(6):
                    w = min(P, 688 - q * P)
                    e.dma_start(srow[0:w, q, :], src[q * P:q * P + w]).then_inc(sf_in, 16)

            e.wait_ge(act_lo, 2 * HEADS)
            e.wait_ge(s_out, 32 * HEADS + 16)
            load_past(0)
            squares(PH["wout"], (0, 1), 1)
            squares(PH["down02"], (0, 1), 2)
            e.wait_ge(evac, PH["win"].group(0, 0) + BANK_CREDIT)
            e.dma_start(r5[:, 0, :], a["lam_re"][0].rearrange("(q g) p -> q (g p)", g=2)).then_inc(in5, 16)
            e.dma_start(r5[:, 1, :], a["lam_im"][0].rearrange("(q g) p -> q (g p)", g=2)).then_inc(in5, 16)
            e.dma_start(r5[:, 2, 0:2], a["log_dt"][0].rearrange("(q g) -> q g", g=2)).then_inc(in5, 16)
            for r, n in enumerate(("bmat_re", "bmat_im")):
                e.dma_start(Bn[:, r], a[n][0].rearrange("(q g) p c -> (g p) q c", g=2)).then_inc(in5, 16)
            for r, n in enumerate(("cmat_re", "cmat_im")):
                e.dma_start(CN[:, r], a[n][0].rearrange("(j g) c p -> (g c) j p", g=8)).then_inc(in5, 16)
            for r, n in enumerate(("state_c_re", "state_c_im")):
                e.dma_start(io5[32 * r:32 * r + 32], a[n][0].rearrange("s (q g) p -> q s (g p)", g=2)).then_inc(in5, 16)
            e.wait_ge(a16, 1)
            e.wait_ge(c5, 10)
            e.wait_ge(x5a, 2 * POOL_PAIRS)
            scan_pairs(gp, st, [(0, POOL_PAIRS // 2), (POOL_PAIRS // 2, POOL_PAIRS)])
            gp.memset(tmp5[:, 0, 0:1], 0.0).then_inc(scan5p, 1)
            e.wait_ge(y5v, 8)
            e.wait_ge(out_dma, 16 * (STORES_A + STORES_F + STORES_C))
            load_past(1)
            squares(PH["glu"], (1, 3), 3)
            squares(PH["down12"], (0, 1), 4)

        @block.vector
        def _(e):
            v = nc.vector
            st = Steps(e, dchain)

            def split_tile(ph, i, j):
                e.wait_ge(rounded, ph.tile(i, j) + 1 + RING)
                v.tensor_tensor(wl[:, j % RING, :], raw[:, j % RING, :], wh[:, j % RING, :].bitcast(F32), ALU.subtract) \
                    .then_inc(split, 1)

            def multiplied(ph, i, j):
                e.wait_ge(used, ph.tile(i, j) + 1 + CREDIT)

            def lo_of_x(c, g, hn):
                e.wait_ge(h_hi, hn)
                hi = part(h, c, 0).bitcast(F32)
                v.scalar_tensor_tensor(out=part(h, c, 1), in0=one(X, c), scalar=prm[:, ds(c + g, 1)], in1=hi,
                                       op0=ALU.mult, op1=ALU.subtract).then_inc(h_lo, 1)

            def norm_inverse(n):
                e.wait_ge(ms_done, n + 1)
                st.then(v.tensor_scalar(rs[:], BO[:, 0:T], 1.0 / D, EPS, ALU.mult, ALU.add))
                v.reciprocal(rs[:], rs[:]).then_inc(ms_inv, 1)
                e.wait_ge(rstd, n + 1)

            v.memset(tiny[:, 11, 0:1], 0.0).then_inc(split, CREDIT)
            v.memset(tiny[:, 11, 1:2], 0.0).then_inc(used, CREDIT)
            v.memset(tiny[:, 11, 2:3], 0.0).then_inc(evac, BANK_CREDIT)
            v.memset(tiny[:, 11, 3:4], 0.0).then_inc(a_ready, 2)
            v.memset(tiny[:, 11, 4:5], 0.0).then_inc(a_used, 2)
            v.memset(tiny[:, 11, 5:6], 0.0).then_inc(s_out, 16)
            v.memset(ones[:], 1.0)
            for c in range(DC):
                e.wait_ge(x_t, c + 1)
                v.tensor_copy(X[:, c, :], bank[c % 2][:, 0:T]).then_inc(x_c, 1)
            e.wait_ge(rows_t, 9)
            e.wait_ge(x_t, DC)
            v.memset(XA[:, 0:3], 0.0)
            v.memset(D1[:], 0.0)
            st.then(v.memset(EN[:], 0.0))
            v.memset(EN[:, CH - 1:TP:CH], 1.0)
            v.memset(EN[:, TP + LS - 1:T:LS], 1.0)
            v.memset(KM[:], 0.0)
            v.memset(KM3[:], 0.0)
            v.memset(FM[:, T:T + 1], 0.0).then_inc(once, 1)
            for c in range(DC):
                e.wait_ge(h_hi, c + 1)
                v.scalar_tensor_tensor(out=h[:, c, 1, :], in0=X[:, c, :], scalar=col("g_mix", c), in1=h[:, c, 0, :].bitcast(F32),
                                       op0=ALU.mult, op1=ALU.subtract).then_inc(h_lo, 1)
            lam = prm[:, COL["lam_a"]:COL["lam_a"] + HEADS]
            lb = prm[:, COL["lb"]:COL["lb"] + HEADS]
            e.wait_ge(rows_c, 9)
            st.then(v.scalar_tensor_tensor(out=tiny[:, 3, :], in0=lam, scalar=-1.0, in1=lam, op0=ALU.mult, op1=ALU.max))
            v.tensor_tensor(tiny[:, 5, :], lb, lb, ALU.subtract).then_inc(lam_v, 1)
            e.wait_ge(lam_a, 1)
            st.then(v.tensor_scalar(tiny[:, 7, :], tiny[:, 4, :], 2.0, None, ALU.add))
            st.then(v.reciprocal(tiny[:, 7, :], tiny[:, 7, :]))
            st.then(v.tensor_tensor(tiny[:, 7, :], tiny[:, 7, :], tiny[:, 4, :], ALU.mult))
            st.then(v.tensor_tensor(tiny[:, 8, :], tiny[:, 7, :], tiny[:, 7, :], ALU.mult))
            st.then(v.tensor_scalar(tiny[:, 9, :], tiny[:, 8, :], 1.0 / 17, None, ALU.mult))
            for m in (15, 13, 11, 9, 7, 5, 3):
                st.then(v.scalar_tensor_tensor(out=tiny[:, 9, :], in0=tiny[:, 9, :], scalar=1.0 / m, in1=tiny[:, 8, :],
                                               op0=ALU.add, op1=ALU.mult))
            st.then(v.scalar_tensor_tensor(out=tiny[:, 9, :], in0=tiny[:, 9, :], scalar=1.0, in1=tiny[:, 7, :],
                                           op0=ALU.add, op1=ALU.mult))
            st.then(v.tensor_scalar(tiny[:, 10, :], lam, -1.0, 0.0, ALU.mult, ALU.max))
            st.then(v.scalar_tensor_tensor(out=tiny[:, 9, :], in0=tiny[:, 9, :], scalar=2.0, in1=tiny[:, 10, :],
                                           op0=ALU.mult, op1=ALU.add))
            st.then(v.tensor_scalar(rate, tiny[:, 9, :], -C_RG, None, ALU.mult))
            st.then(v.reciprocal(tiny[:, 5, :], tiny[:, 6, :]))
            st.then(v.tensor_tensor(tiny[:, 5, :], tiny[:, 5, :], tiny[:, 6, :], ALU.mult))
            st.then(v.tensor_tensor(tiny[:, 5, :], tiny[:, 5, :], tiny[:, 5, :], ALU.subtract))
            st.then(v.tensor_scalar(tiny[:, 5, :], tiny[:, 5, :], 0.0, 1.0, ALU.max, ALU.min))
            st.then(v.tensor_scalar(lbm, tiny[:, 5, :], 1e-30, None, ALU.max))
            st.then(v.tensor_scalar(oml, tiny[:, 5, :], -1.0, 1.0, ALU.mult, ALU.add))
            for j in range(RING):
                e.wait_ge(rounded, j + 1)
                v.tensor_tensor(wl[:, j, :], raw[:, j, :], wh[:, j, :].bitcast(F32), ALU.subtract).then_inc(split, 1)
            norm_inverse(0)

            ph = PH["head"]

            def take(i, dst, r):
                multiplied(ph, i, 2 * r + 1)
                v.tensor_tensor(dst, bank[ph.bank(r)][:, 0:T], rs[:], ALU.mult).then_inc(evac, 1)
                e.wait_ge(evac, ph.group(i, r) + 1 + BANK_CREDIT)

            def head(i, ended):
                n = i + 1

                def band(d):
                    w = CH - d
                    e.wait_ge(a_ready, i * CH + (d + 3))
                    wt = BA[d % 2][:, 0:NCH * w].rearrange("p (c w) -> p c w", w=w)
                    vals = bands(V, 0)[:, :, 0:w]
                    if d == 0:
                        if ended:
                            e.wait_ge(act_lo, i * 2)
                        v.tensor_tensor(bands(OB, 0), wt, vals, ALU.mult).then_inc(a_used, 1)
                        e.wait_ge(a_used, i * CH + (d + 3))
                    else:
                        v.tensor_tensor(W[:, 0:NCH * w].rearrange("p (c w) -> p c w", w=w), wt, vals, ALU.mult).then_inc(a_used, 1)
                        e.wait_ge(a_used, i * CH + (d + 3))
                        st.then(v.tensor_tensor(bands(OB, d), bands(OB, d), W[:, 0:NCH * w].rearrange("p (c w) -> p c w", w=w), ALU.add))

                for j in range(12):
                    if ended and j == 0:
                        end_of(i - 1, -1)
                    for d in BANDS.get(j, ()):
                        band(d)
                    split_tile(ph, i, j)
                    if ended:
                        end_of(i - 1, j)
                    if j == 1:
                        take(i, Q[:], 0)
                    if j == 3:
                        take(i, FZ[:], 1)
                        e.wait_ge(sk, n)
                        st.then(v.tensor_scalar(FM[:, 0:T], FM[:, 0:T], tiny[:, 2, ds(i, 1)], tiny[:, 1, ds(i, 1)], ALU.mult, ALU.add))
                        st.then(v.tensor_scalar(K[:], K[:], tiny[:, 2, ds(i, 1)], None, ALU.mult))
                        v.tensor_copy(D1[:, 0:TP:CH], FM[:, 0:TP:CH])
                        st.then(v.tensor_copy(D1[:, TP:T:LS], FM[:, TP:T:LS]))
                        v.memset(FM[:, 0:TP:CH], 0.0)
                        v.memset(FM[:, TP:T:LS], 0.0).then_inc(bandin, 1)
                        e.wait_ge(bandin, n)
                        v.tensor_tensor_scan(FZ[:, ::-1], FM[:, 1:T + 1][:, ::-1], EN[:, ::-1], 0.0, ALU.mult, ALU.add).then_inc(sfx, 1)
                    if j == 5:
                        st.then(v.tensor_tensor_scan(QF[:], FM[:, 0:T], D1[:], 0.0, ALU.mult, ALU.add))
                        v.tensor_copy(FE[:, 0:PCH], QF[:, CH - 1:TP:CH])
                        st.then(v.tensor_copy(FE[:, PCH:UNITS], QF[:, TP + LS - 1:T:LS]))
                        st.then(v.tensor_tensor(QF[:], QF[:], Q[:], ALU.mult))
                    if j == 5:
                        take(i, V[:], 2)
                    if j == 7:
                        multiplied(ph, i, 7)
                        pv = bank[ph.bank(3)][:, 0:T]
                        v.tensor_tensor(XA[:, 3:3 + TP], pv[:, 0:TP], rs[:, 0:TP], ALU.mult)
                        v.tensor_tensor(XAs[:, :, 3:3 + LS], samples(pv), samples(rs), ALU.mult).then_inc(evac, 1)
                        past = prm[:, COL["a_conv"]:COL["a_conv"] + 192].rearrange("p (s r c) -> p s r c", r=3, c=HEADS)
                        v.tensor_copy(XAs[:, :, 0:3], past[:, :, :, ds(i, 1)].rearrange("p s r c -> p s (r c)")).then_inc(conv_in, 1)
                        e.wait_ge(conv_in, n)
                        v.tensor_copy(ncva[:, 0, :, ds(i, 1)].rearrange("p r c -> p (r c)"), XA[:, TP:TP + 3])
                        v.tensor_copy(ncva[:, 1:1 + NS, :, ds(i, 1)].rearrange("p s r c -> p s (r c)"), XAs[:, :, LS:LS + 3])
                        e.wait_ge(ct, n)
                        for k in (2, 1):
                            st.then(v.scalar_tensor_tensor(out=CT[:, 0:360], in0=XA[:, k:k + 360], scalar=dcol("conv_a_w", i, 8 * k),
                                                           in1=CT[:, 0:360], op0=ALU.mult, op1=ALU.add))
                        v.scalar_tensor_tensor(out=XC[:, 0:TP], in0=XA[:, 0:TP], scalar=dcol("conv_a_w", i), in1=CT[:, 0:TP],
                                               op0=ALU.mult, op1=ALU.add)
                        v.scalar_tensor_tensor(out=samples(XC), in0=XAs[:, :, 0:LS], scalar=dcol("conv_a_w", i),
                                               in1=CTs[:, :, 0:LS], op0=ALU.mult, op1=ALU.add).then_inc(xc, 1)
                    if j == 9:
                        take(i, GB[:], 4)
                    if j == 9:
                        e.wait_ge(sbg, n)
                        st.then(v.scalar_tensor_tensor(out=GB[:], in0=GB[:], scalar=dcol("gn_b", i), in1=SB[:],
                                                       op0=ALU.mult, op1=ALU.mult))
                    if j == 10:
                        e.wait_ge(th, n)
                        st.then(v.tensor_tensor(RT[:], AA[:], AA[:], ALU.mult))
                        v.scalar_tensor_tensor(out=RT[:], in0=RT[:], scalar=1.0, in1=CT[:, 0:T], op0=ALU.add, op1=ALU.mult) \
                            .then_inc(t_in, 1)

            def chain(i, units):
                for u in units:
                    e.wait_ge(s_done, i * (UNITS + 1) + (u + 1))
                    if u % 4 == 0:
                        e.wait_ge(u_ready, i * 7 + (u // 4 + 1))
                    if u < PCH:
                        old, new = SR[:, u % 8, :], SR[:, (u + 1) % 8, :]
                        if u >= 7:
                            e.wait_ge(inter, i * UNITS + (NS + u - 6))
                    else:
                        old = new = SS[:, u - PCH, :]
                    v.scalar_tensor_tensor(out=new, in0=old, scalar=FE[:, u:u + 1],
                                           in1=BM[u // 4 % 2][:, u % 4 * P:(u % 4 + 1) * P], op0=ALU.mult, op1=ALU.add) \
                        .then_inc(s_done, 1)

            def end_of(i, j):
                n = i + 1
                if j == -1:
                    take(i, GA[:], 5)
                    e.wait_ge(s_out, i * 32 + 16)
                    v.memset(SR[:, 0, :], 0.0).then_inc(s_done, 1)
                    chain(i, range(0, 4))
                if j == 0:
                    chain(i, range(4, 12))
                if j == 1:
                    e.wait_ge(b_ready, n)
                    h0 = prm[:, COL["a_h"]:COL["a_h"] + 64].rearrange("p (s c) -> p s c", c=HEADS)[:, :, ds(i, 1)].rearrange("p s c -> p (s c)")
                    st.then(v.tensor_tensor(HH[:, 0:NS], AA[:, TP:T:LS], h0, ALU.mult))
                    st.then(v.tensor_tensor(IG[:, TP:T:LS], IG[:, TP:T:LS], HH[:, 0:NS], ALU.add))
                    st.then(v.memset(AA[:, TP:T:LS], 0.0))
                    st.then(v.tensor_tensor_scan(HH[:], AA[:], IG[:], 0.0, ALU.mult, ALU.add))
                    v.tensor_copy(hlast[:, 0, ds(i, 1)], HH[:, TP - 1:TP])
                    st.then(v.tensor_copy(hlast[:, 1:1 + NS, ds(i, 1)].rearrange("p s c -> p (s c)"), HH[:, TP + LS - 1:T:LS]))
                    e.wait_ge(ga, n)
                    v.tensor_tensor(HH[:], HH[:], GA[:], ALU.mult).then_inc(oa, 1)
                if j == 2:
                    chain(i, range(12, 16))
                if j == 3:
                    e.wait_ge(act_hi, i * 2 + 1)
                    v.tensor_tensor(part(act, i * 2, 1), HH[:], part(act, i * 2, 0).bitcast(F32), ALU.subtract).then_inc(act_lo, 1)
                    chain(i, range(16, 24))
                if j == 4:
                    chain(i, range(24, UNITS))
                    e.wait_ge(inter, n * UNITS)
                    st.then(v.tensor_tensor(OB[:], OB[:], BO[:, 0:T], ALU.add))
                    v.tensor_tensor(W[:], OB[:], OB[:], ALU.mult).then_inc(oo, 1)
                if j == 5:
                    e.wait_ge(oms, n)
                    st.then(v.tensor_scalar(SB[:], BM[1][:, 0:T], 1.0 / P, EPS, ALU.mult, ALU.add))
                    v.reciprocal(SB[:], SB[:]).then_inc(oinv, 1)
                if j == 6:
                    e.wait_ge(osq, n)
                    st.then(v.tensor_tensor(OB[:], OB[:], SB[:], ALU.mult))
                    v.tensor_tensor(OB[:], OB[:], GB[:], ALU.mult).then_inc(ob, 1)
                    e.wait_ge(act_hi, i * 2 + 2)
                    v.tensor_tensor(part(act, i * 2 + 1, 1), OB[:], part(act, i * 2 + 1, 0).bitcast(F32), ALU.subtract).then_inc(act_lo, 1)

            head(0, False)
            with e.Fori(1, HEADS) as i:
                st.enter(i, DVE_HEAD, 1)
                head(i, True)
                st.leave(HEADS)
            for j in range(-1, 7):
                end_of(HEADS - 1, j)

            def add_to_x(ph, i, r, j, g, norm):
                c = i * 2 + r
                multiplied(ph, i, j)
                v.tensor_tensor(one(X, c), one(X, c), bank[ph.bank(r)][:, 0:T], ALU.add).then_inc(evac, 1)
                if g is not None:
                    lo_of_x(c, g, i * 2 + (norm * DC + r + 1))

            ph = PH["wout"]
            with e.Fori(0, ph.bodies) as i:
                for j in range(4):
                    split_tile(ph, i, j)
                    if j % 2:
                        add_to_x(ph, i, j // 2, j, COL["g_ffn"], 1)

            def ffn(l, gnext, norm_next):
                if l == 0:
                    e.wait_ge(nc_t, 3)
                e.wait_ge(s_out, 32 * HEADS + 16)
                v.memset(UP[:, 0:2], 0.0)
                norm_inverse(NORMS[f"up{l}0"])
                e.wait_ge(sf_c, 6 * (l + 1))
                for p, (f0, n) in enumerate(PARTS):
                    ph = PH[f"up{l}{p}"]
                    cc = l * FFC + f0
                    slots = 16 + l * 8 + cc
                    w = lambda i, k: dcol("conv_f_w", i, (l * 3 + k) * FFC + f0)
                    with e.Fori(0, n) as i:
                        st.enter(i, 1)
                        for j in range(4):
                            split_tile(ph, i, j)
                            if j == 1:
                                multiplied(ph, i, 1)
                                pv = bank[0][:, 0:T]
                                v.tensor_tensor(UP[:, 2:2 + TP], pv[:, 0:TP], rs[:, 0:TP], ALU.mult)
                                v.tensor_tensor(UPs[:, :, 2:2 + LS], samples(pv), samples(rs), ALU.mult).then_inc(evac, 1)
                                v.tensor_copy(UPs[:, :, 0:2], SF.rearrange("p (s r) f -> p s r f", r=2)[:, :, :, ds(i + f0, 1)]
                                              .rearrange("p s r f -> p s (r f)")).then_inc(up_in, 1)
                                e.wait_ge(up_in, i + (cc + 1))
                                v.tensor_copy(NCF[:, 0, :, ds(i + f0, 1)].rearrange("p r f -> p (r f)"), UP[:, TP:TP + 2])
                                v.tensor_copy(NCF[:, 1:1 + NS, :, ds(i + f0, 1)].rearrange("p s r f -> p s (r f)"), UPs[:, :, LS:LS + 2])
                                e.wait_ge(cv0, i + (cc + 1))
                                st.then(v.scalar_tensor_tensor(out=CV[:, 0:UPW - 2], in0=UP[:, 1:UPW - 1], scalar=w(i, 1),
                                                               in1=CV[:, 0:UPW - 2], op0=ALU.mult, op1=ALU.add))
                                v.scalar_tensor_tensor(out=CV[:, 0:UPW - 2], in0=UP[:, 0:UPW - 2], scalar=w(i, 0),
                                                       in1=CV[:, 0:UPW - 2], op0=ALU.mult, op1=ALU.add).then_inc(cv2, 1)
                            if j == 3:
                                multiplied(ph, i, 3)
                                v.tensor_tensor(GT[:], bank[1][:, 0:T], rs[:], ALU.mult).then_inc(evac, 1)
                                e.wait_ge(evac, ph.group(i, 1) + 1 + BANK_CREDIT)
                                e.wait_ge(gelu, i + (cc + 1))
                                v.tensor_tensor(AC[:, 0:TP], GT[:, 0:TP], CV[:, 0:TP], ALU.mult)
                                v.tensor_tensor(samples(AC), samples(GT), CVs[:, :, 0:LS], ALU.mult).then_inc(prod, 1)
                                e.wait_ge(prod, i + (cc + 1))
                                e.wait_ge(act_hi, i + (slots + 1))
                                v.tensor_tensor(part(act, i, 1), AC[:], part(act, i, 0).bitcast(F32), ALU.subtract).then_inc(act_lo, 1)
                        st.leave(n)
                    ph = PH[f"down{l}{p}"]
                    last = p == len(PARTS) - 1
                    g = gnext if last else None
                    end = last and l == 1
                    with e.Fori(0, ph.bodies - end) as i:
                        for j in range(4):
                            split_tile(ph, i, j)
                            if j % 2:
                                add_to_x(ph, i, j // 2, j, g, norm_next)
                    if end:
                        for r in range(2):
                            add_to_x(ph, ph.bodies - 1, r, 2 * r + 1, None, norm_next)
                v.tensor_copy(NCF[:, 0, 0, 0:1], NCF[:, 0, 0, 0:1]).then_inc(nc_v, 1)

            ffn(0, COL["g_mix"] + DC, 2)
            norm_inverse(NORMS["win"])

            e.wait_ge(out_dma, 16 * (STORES_A + STORES_F))
            ph = PH["win"]
            with e.Fori(0, 2) as i:
                for j in range(4):
                    split_tile(ph, i, j)
                    if j % 2:
                        multiplied(ph, i, j)
                        v.tensor_tensor(one(U5, i * 2 + j // 2), bank[ph.bank(j // 2)][:, 0:T], rs[:], ALU.mult).then_inc(evac, 1)

            R = lambda k: r5[:, k, :]
            e.wait_ge(in5, 16 * 9)
            v.memset(BX[:], 0.0)
            v.tensor_copy(r5[:, 14, 0:1], r5[:, 2, 0:1]).then_inc(a5v, 1)
            e.wait_ge(a5a, 1)
            for g in range(2):
                sl = slice(g * P5, (g + 1) * P5)
                v.tensor_scalar(r5[:, 5, sl], r5[:, 0, sl], r5[:, 3, g:g + 1], None, ALU.mult)
                ins = v.tensor_scalar(r5[:, 7, sl], r5[:, 1, sl], r5[:, 3, g:g + 1], None, ALU.mult)
            ins.then_inc(a5v, 1)
            e.wait_ge(a5v, 2)
            magic = 1.5 * 2.0 ** 23
            st.then(v.tensor_scalar(R(8), R(7), float(1 / (2 * np.pi)), magic, ALU.mult, ALU.add))
            st.then(v.tensor_scalar(R(8), R(8), magic, None, ALU.subtract))
            c1 = 6.28125
            c2 = float(np.float32(np.round((2 * np.pi - c1) * 2 ** 21) / 2 ** 21))
            c3 = float(2 * np.pi - c1 - c2)
            st.then(v.scalar_tensor_tensor(out=R(9), in0=R(8), scalar=-c1, in1=R(7), op0=ALU.mult, op1=ALU.add))
            st.then(v.scalar_tensor_tensor(out=R(9), in0=R(8), scalar=-c2, in1=R(9), op0=ALU.mult, op1=ALU.add))
            st.then(v.scalar_tensor_tensor(out=R(9), in0=R(8), scalar=-c3, in1=R(9), op0=ALU.mult, op1=ALU.add))
            pi = float(np.nextafter(np.float32(np.pi), np.float32(0)))
            v.tensor_scalar(R(9), R(9), pi, -pi, ALU.min, ALU.max).then_inc(a5v, 1)
            e.wait_ge(a5a, 3)
            st.then(v.tensor_tensor(R(11), R(11), R(11), ALU.mult))
            st.then(v.tensor_scalar(R(11), R(11), -2.0, 1.0, ALU.mult, ALU.add))
            st.then(v.tensor_tensor(R(12), R(6), R(11), ALU.mult))
            st.then(v.tensor_tensor(R(13), R(6), R(10), ALU.mult))
            st.then(v.tensor_tensor(R(14), R(0), R(0), ALU.mult))
            st.then(v.tensor_tensor(R(15), R(1), R(1), ALU.mult))
            st.then(v.tensor_tensor(R(14), R(14), R(15), ALU.add))
            st.then(v.reciprocal(R(14), R(14)))
            st.then(v.scalar_tensor_tensor(out=R(8), in0=R(12), scalar=-1.0, in1=R(0), op0=ALU.add, op1=ALU.mult))
            st.then(v.tensor_tensor(R(9), R(13), R(1), ALU.mult))
            st.then(v.tensor_tensor(R(8), R(8), R(9), ALU.add))
            st.then(v.tensor_tensor(R(8), R(8), R(14), ALU.mult))
            st.then(v.tensor_tensor(R(9), R(13), R(0), ALU.mult))
            st.then(v.scalar_tensor_tensor(out=R(10), in0=R(12), scalar=-1.0, in1=R(1), op0=ALU.add, op1=ALU.mult))
            st.then(v.tensor_tensor(R(9), R(9), R(10), ALU.subtract))
            v.tensor_tensor(R(9), R(9), R(14), ALU.mult).then_inc(a5v, 1)
            for r in range(2):
                for g in range(2):
                    ins = v.tensor_scalar(CX[:, r].rearrange("p j (g x) -> p j g x", g=2)[:, :, g, :], CN[:, r],
                                          masks[:, 2 * r + g:2 * r + g + 1], None, ALU.mult)
            ins.then_inc(a5v, 1)

            with e.Fori(2, ph.bodies) as i:
                for j in range(4):
                    split_tile(ph, i, j)
                    if j % 2:
                        multiplied(ph, i, j)
                        v.tensor_tensor(one(U5, i * 2 + j // 2), bank[ph.bank(j // 2)][:, 0:T], rs[:], ALU.mult).then_inc(evac, 1)

            e.wait_ge(t5, 1)
            az = BM[0][:, 0:4 * PAIRS].rearrange("p (k n) -> p k n", k=4)
            v.tensor_copy(A5[:, 0, 0, :], az[:, 0, :])
            v.tensor_copy(A5[:, 0, 1, :], az[:, 0, :])
            v.tensor_scalar(A5[:, 1, 0, :], az[:, 1, :], -1.0, None, ALU.mult)
            v.tensor_copy(A5[:, 1, 1, :], az[:, 1, :])
            v.tensor_copy(zz[:, 0:2, :], az[:, 2:4, :]).then_inc(c5, 1)
            e.wait_ge(c5, 1)
            re, im, tr, ti, t2 = A16[:, 0, 0, :], A16[:, 1, 1, :], zz[:, 2, :], zz[:, 3, :], A16[:, 1, 0, :]
            v.tensor_copy(re, A5[:, 0, 0, :])
            st.then(v.tensor_copy(im, A5[:, 1, 1, :]))
            for _ in range(4):
                v.tensor_tensor(tr, re, re, ALU.mult)
                v.tensor_tensor(ti, im, im, ALU.mult)
                st.then(v.scalar_tensor_tensor(out=t2, in0=re, scalar=2.0, in1=im, op0=ALU.mult, op1=ALU.mult))
                v.tensor_tensor(re, tr, ti, ALU.subtract)
                st.then(v.tensor_copy(im, t2))
            v.tensor_copy(A16[:, 0, 1, :], re)
            v.tensor_scalar(A16[:, 1, 0, :], im, -1.0, None, ALU.mult).then_inc(a16, 1)
            e.wait_ge(a16, 1)
            zb = lambda k: zz[:, k, :].unsqueeze(2).to_broadcast([P, PAIRS, C5])
            v.tensor_tensor(B2[:, 0], Bn[:, 0], zb(0), ALU.mult)
            st.then(v.tensor_tensor(B2[:, 1], Bn[:, 1], zb(1), ALU.mult))
            st.then(v.tensor_tensor(B2[:, 0], B2[:, 0], B2[:, 1], ALU.subtract))
            st.then(v.tensor_tensor(B2[:, 1], Bn[:, 1], zb(0), ALU.mult))
            st.then(v.tensor_tensor(Bn[:, 0], Bn[:, 0], zb(1), ALU.mult))
            st.then(v.tensor_tensor(B2[:, 1], B2[:, 1], Bn[:, 0], ALU.add))
            for r in range(2):
                for g in range(2):
                    rowsl = slice(g * P5, (g + 1) * P5)
                    ins = v.tensor_copy(BX[rowsl, r].rearrange("p j (q g c) -> p (j q) g c", q=4, g=2)[:, :, g, :], B2[rowsl, r])
            ins.then_inc(a5v, 1)
            for b in range(8):
                dst = (CTm if b < 4 else BTm)[:, b % 2 * 4:b % 2 * 4 + 4, b % 4 // 2, :]
                e.wait_ge(t5, b + 2)
                v.tensor_copy(dst, BM[(b + 1) % 2][:].rearrange("p (j n) -> p j n", j=4)).then_inc(c5, 1)
            e.wait_ge(t5, 10)
            v.tensor_copy(st5.rearrange("p s r k -> p (s r k)"), BM[1][:]).then_inc(c5, 1)
            e.wait_ge(c5, 10)
            e.wait_ge(x5a, 2 * PAIRS)
            scan_pairs(v, st, [(POOL_PAIRS, MID_PAIR), (MID_PAIR, PAIRS)])
            v.memset(tiny[:, 11, 6:7], 0.0).then_inc(scan5, 1)
            e.wait_ge(scan5p, 1)
            v.tensor_copy(fin5[:, 0], xs[:, :, :, TP - 1])
            v.tensor_copy(fin5[:, 1:1 + NS].rearrange("p s r q -> p r q s"), xs[:, :, :, TP + LS - 1:T:LS]).then_inc(scan5, 1)
            for k, c in enumerate(YORDER):
                if k >= 2:
                    e.wait_ge(act_lo, 16 + FFC + k - 1)
                e.wait_ge(y5, k + 1)
                v.scalar_tensor_tensor(out=ys5[:, k % 2], in0=U5[:, c, :], scalar=col("d_skip", c), in1=bank[YBANK[k]][:, 0:T],
                                       op0=ALU.mult, op1=ALU.add).then_inc(y5v, 1)
                e.wait_ge(act_hi, 16 + FFC + k + 1)
                v.tensor_tensor(act[:, c, 1, :], ys5[:, k % 2], act[:, c, 0, :].bitcast(F32), ALU.subtract).then_inc(act_lo, 1)

            ph = PH["glu"]
            with e.Fori(0, ph.bodies) as i:
                st.enter(i, 2)
                for j in range(4):
                    split_tile(ph, i, j)
                    if j % 2:
                        c = i * 2 + j // 2
                        e.wait_ge(gsig, i * 2 + (j // 2 + 1))
                        st.then(v.tensor_tensor(VT[:], bank[j - 1][:, 0:T], GS[:], ALU.mult))
                        v.tensor_tensor(one(X, c), one(X, c), VT[:], ALU.add).then_inc(evac, 2)
                        lo_of_x(c, COL["g_ffn"] + DC, i * 2 + (3 * DC + j // 2 + 1))
                st.leave(ph.bodies)
            ffn(1, None, 4)
            norm_inverse(NORMS["final"])
            for c in range(DC):
                if c >= 2:
                    e.wait_ge(y_t, c - 1)
                v.scalar_tensor_tensor(out=yg[:, c % 2, :], in0=X[:, c, :], scalar=col("g_final", c), in1=rs[:],
                                       op0=ALU.mult, op1=ALU.mult).then_inc(yg_done, 1)

        @block.tensor
        def _(e):
            pe = nc.tensor

            def tile(ph, i, j, kn, x, b, first, last, halfway=None, t0=0):
                e.wait_ge(split, ph.tile(i, j) + 1 + CREDIT)
                slot, out = j % RING, bank[b][:, t0:T]
                for k in range(kn):
                    hi, lo = (half[:, t0:T] for half in x(k))
                    whi, wlo = wh[:, slot, k * P:(k + 1) * P], wl[:, slot, k * P:(k + 1) * P]
                    pe.matmul(out, whi, hi, start=first and k == 0, stop=False)
                    pe.matmul(out, whi, lo, start=False, stop=False)
                    ins = pe.matmul(out, wlo, hi, start=False, stop=last and k == kn - 1)
                    if halfway is not None and k == kn // 2 - 1:
                        halfway()
                ins.then_inc(used, 1)

            def free(ph, i, r):
                e.wait_ge(evac, ph.group(i, r) + (1 + BANK_CREDIT - ph.banks))

            def from_h(k0):
                return lambda k: (h[:, k0 + k, 0, :], h[:, k0 + k, 1, :])

            def from_act(k0):
                return lambda k: (act[:, k0 + k, 0, :], act[:, k0 + k, 1, :])

            def mean_squares(n):
                e.wait_ge(ssq_added, (n + 1) * DC)
                pe.matmul(BO[:, 0:T], ones[:], ssq[:], start=True, stop=True).then_inc(ms_done, 1)

            e.wait_ge(consts_in, 32)
            e.wait_ge(rows_in, 16 * 18)
            for q in range(9):
                w = (80, 86, 86, 86, 86, 88, 64, 96, 96)[q]
                if q >= 2:
                    e.wait_ge(rows_c, q - 1)
                pe.transpose(BM[q % 2][:, 0:w], rows[0:w, q, :], ident[0:w, 0:w]).then_inc(rows_t, 1)
            e.wait_ge(x_in, 80)
            for c in range(DC):
                if c >= 2:
                    e.wait_ge(x_c, c - 1)
                for t in range(3):
                    n = (P, P, T - 2 * P)[t]
                    ins = pe.transpose(bank[c % 2][:, t * P:t * P + n], xin[0:n, t, c * P:(c + 1) * P], ident[0:n, 0:n])
                ins.then_inc(x_t, 1)
            e.wait_ge(once, 1)
            mean_squares(0)
            e.wait_ge(h_lo, DC)

            ph = PH["head"]

            def band(i, d):
                w = CH - d
                e.wait_ge(p_ready, i * CH + (d + 1))
                e.wait_ge(a_used, i * CH + (d + 1))
                pe.matmul(BA[d % 2][:, 0:NCH * w], ones[:], PB[:, d % 2, 0:NCH * w], start=True, stop=True).then_inc(a_ready, 1)

            def updates(i, b):
                if b < 2:
                    e.wait_ge(gates_read, i + 1)
                else:
                    e.wait_ge(s_done, i * (UNITS + 1) + (4 * (b - 2) + 5))
                row = None
                for u in range(4 * b, min(4 * b + 4, UNITS)):
                    out = BM[b % 2][:, u % 4 * P:(u % 4 + 1) * P]
                    if u < PCH - 1:
                        t, r0, vers = u // 8, 32 * (u % 8 // 2), [(u // 8) * 2 + u % 2]
                        rn = 32
                    else:
                        t, off = 2, (0 if u == PCH - 1 else CH + LS * (u - PCH))
                        r0, rn = off // 32 * 32, min(32, 80 - off // 32 * 32)
                        vers = [4, 5] if u == PCH - 1 else [4 + off % 32 // 8]
                    if row not in (None, r0):
                        ins.then_inc(row_turn, 1)
                        e.wait_ge(row_turn, i * ROW_TURNS + (b + 1))
                    row = r0
                    for m, k in enumerate(vers):
                        ins = pe.matmul(out, TK[r0:r0 + rn, k, :], TV[r0:r0 + rn, t, :], start=m == 0, stop=m == len(vers) - 1)
                ins.then_inc(u_ready, 1)

            def with_state(i, us):
                for u in us:
                    if u < PCH:
                        e.wait_ge(s_done, i * (UNITS + 1) + (u + 1))
                        c0, w, S = u * CH, CH, SR[:, u % 8, :]
                    else:
                        c0, w, S = TP + (u - PCH) * LS, LS, SS[:, u - PCH, :]
                    pe.matmul(BO[:, c0:c0 + w], S, QF[:, c0:c0 + w], start=True, stop=True).then_inc(inter, 1)

            def head(i, ended):
                n = i + 1
                for j in range(12):
                    if j % 2 == 0:
                        free(ph, i, j // 2)
                    tile(ph, i, j, 8, from_h(8 * (j % 2)), ph.bank(j // 2), j % 2 == 0, j % 2 == 1,
                         (lambda: band(i, BANDS[j][0])) if j in BANDS else None)
                    for d in BANDS.get(j, ())[1:]:
                        band(i, d)
                    if ended:
                        end_of(i - 1, j)
                    if j == 8:
                        e.wait_ge(km, n)
                        for k in range(4):
                            ins = pe.transpose(BM[0][:, k * P:(k + 1) * P], KM[:, k % 2, k // 2 * P:(k // 2 + 1) * P], ident[:])
                        ins.then_inc(kt, 1)
                        for k in range(4):
                            ins = pe.transpose(BM[1][0:80, k * P:(k + 1) * P], KM3[:, k, 0:80], ident[:])
                        ins.then_inc(kt, 1)
                        for k in range(3):
                            w = min(P, T - k * P)
                            ins = pe.transpose(BO[0:w, k * P:(k + 1) * P], V[:, k * P:k * P + w], ident[:])
                        ins.then_inc(kt, 1)
                    if j == 9:
                        e.wait_ge(tk_copied, i * 3 + 2)
                        e.wait_ge(xc, n)
                        e.wait_ge(wr_in, n * 32)
                        pe.matmul(BM[0][:, 0:T], WR[:, 0, :], XC[:], start=True, stop=True)
                        pe.matmul(BM[1][:, 0:T], WR[:, 1, :], XC[:], start=True, stop=True).then_inc(gates, 1)
                    if j == 10:
                        e.wait_ge(tk_copied, i * 3 + 3)
                        updates(i, 0)
                        updates(i, 1)

            def end_of(i, j):
                if j == 0:
                    e.wait_ge(ss_in, (i + 1) * 16)
                    with_state(i, range(PCH, UNITS))
                if j < 5:
                    with_state(i, range(4 * j, min(4 * j + 4, PCH)))
                    updates(i, j + 2)
                if j == 5:
                    e.wait_ge(oo, i + 1)
                    pe.matmul(BM[1][:, 0:T], ones[:], W[:], start=True, stop=True).then_inc(oms, 1)

            head(0, False)
            with e.Fori(1, HEADS) as i:
                head(i, True)
            for j in range(6):
                end_of(HEADS - 1, j)

            mixed = lambda k0: (lambda k: (act[:, (2 * (k0 + k)) if k0 + k < 8 else (2 * (k0 + k - 8) + 1), 0, :],
                                           act[:, (2 * (k0 + k)) if k0 + k < 8 else (2 * (k0 + k - 8) + 1), 1, :]))
            e.wait_ge(act_lo, 2 * HEADS)
            ph = PH["wout"]
            with e.Fori(0, ph.bodies) as i:
                for j in range(4):
                    if j % 2 == 0:
                        free(ph, i, j // 2)
                    tile(ph, i, j, 8, mixed(8 * (j % 2)), ph.bank(j // 2), j % 2 == 0, j % 2 == 1)

            flatn = ncva.rearrange("p s r c -> p (s r c)")
            for q, src in enumerate((flatn[:, 0:P], flatn[:, P:216], hlast.rearrange("p s c -> p (s c)"))):
                if q == 2:
                    e.wait_ge(nc_c, 1)
                pe.transpose(BM[q % 2][0:src.shape[1], 0:P], src, ident[:]).then_inc(nc_t, 1)

            def ffn(l):
                e.wait_ge(sf_in, 16 * 6 * (l + 1))
                for q in range(6):
                    w = min(P, 688 - q * P)
                    if q >= 2 or l == 0:
                        e.wait_ge(sf_c, l * 6 + q - 1) if q >= 2 else e.wait_ge(nc_c, 3)
                    pe.transpose(BM[q % 2][:, 0:w], srow[0:w, q, :], ident[0:w, 0:w]).then_inc(sf_t, 1)
                mean_squares(NORMS[f"up{l}0"])
                e.wait_ge(h_lo, DC * (2 if l == 0 else 4))
                for p, (f0, n) in enumerate(PARTS):
                    ph = PH[f"up{l}{p}"]
                    with e.Fori(0, n) as i:
                        for j in range(4):
                            if j % 2 == 0:
                                free(ph, i, j // 2)
                            tile(ph, i, j, 8, from_h(8 * (j % 2)), ph.bank(j // 2), j % 2 == 0, j % 2 == 1, None, l * DEAD)
                    e.wait_ge(act_lo, 16 + l * 8 + l * FFC + f0 + n)
                    ph = PH[f"down{l}{p}"]
                    with e.Fori(0, ph.bodies) as i:
                        for j in range(4):
                            k0, kn = halves(n)[j % 2]
                            if j % 2 == 0:
                                free(ph, i, j // 2)
                            tile(ph, i, j, kn, from_act(k0), ph.bank(j // 2), j % 2 == 0, j % 2 == 1, None, l * DEAD)
                flat = NCF.rearrange("p s r f -> p (s r f)")
                e.wait_ge(nc_v, l + 1)
                for q in range(7):
                    w = min(P, 774 - q * P)
                    if q >= 2:
                        e.wait_ge(nc_c, 3 + l * 7 + q - 1)
                    pe.transpose(BM[q % 2][0:w, 0:P], flat[:, q * P:q * P + w], ident[:]).then_inc(nc_t, 1)

            ffn(0)
            mean_squares(NORMS["win"])
            e.wait_ge(h_lo, 3 * DC)
            ph = PH["win"]
            with e.Fori(0, ph.bodies) as i:
                for j in range(4):
                    if j % 2 == 0:
                        free(ph, i, j // 2)
                    tile(ph, i, j, 8, from_h(8 * (j % 2)), ph.bank(j // 2), j % 2 == 0, j % 2 == 1)

            e.wait_ge(nc_c, 10)
            e.wait_ge(a5v, 5)
            for k, r in enumerate((12, 13, 8, 9)):
                ins = pe.transpose(BM[0][:, k * PAIRS:(k + 1) * PAIRS], r5[:, r, :], ident[0:PAIRS, 0:PAIRS])
            ins.then_inc(t5, 1)
            for b in range(8):
                if b:
                    e.wait_ge(c5, b)
                if b == 4:
                    e.wait_ge(a5v, 6)
                src = (CX if b < 4 else BX)[:, b % 4 // 2]
                for k in range(4):
                    ins = pe.transpose(BM[(b + 1) % 2][:, k * P:(k + 1) * P], src[:, b % 2 * 4 + k, :], ident[:])
                ins.then_inc(t5, 1)
            e.wait_ge(c5, 8)
            e.wait_ge(in5, 16 * 9)
            for s in range(NS):
                ins = pe.transpose(BM[1][:, s * 64:(s + 1) * 64], io5[:, s, :], ident[0:64, 0:64])
            ins.then_inc(t5, 1)
            e.wait_ge(evac, PH["glu"].group(0, 0) + BANK_CREDIT)
            e.wait_ge(c5, 10)
            for k in range(PAIRS):
                j, q = k // 4, k % 4
                for r in range(2):
                    if k >= 2:
                        e.wait_ge(x5a, 2 * (k - 2) + r + 1)
                    pe.matmul((BA if k % 2 == 0 else BM)[r][:, 0:T], BTm[32 * q:32 * q + 32, j, r, :],
                              U5[32 * q:32 * q + 32, j, :], start=True, stop=True).then_inc(x5, 1)
            e.wait_ge(x5a, 2 * PAIRS)
            for k, c in enumerate(YORDER):
                if k == 0:
                    e.wait_ge(scan5p, 1)
                if k == POOL_PAIRS // 4:
                    e.wait_ge(scan5, 1)
                if k >= 6:
                    e.wait_ge(y5v, k - 5)
                for q in range(4):
                    for r in range(2):
                        ins = pe.matmul(bank[YBANK[k]][32 * q:32 * q + 32, 0:T], CTm[:, c, r, 32 * q:32 * q + 32],
                                        xs[:, r, 4 * c + q, :], start=r == 0, stop=r == 1)
                ins.then_inc(y5, 1)
            e.wait_ge(scan5, 2)
            for s in range(9):
                if s >= 2:
                    e.wait_ge(fs_c, s - 1)
                pe.transpose(BM[s % 2][0:2 * PAIRS, 0:P], fin5[:, s].rearrange("p r q -> p (r q)"), ident[:]).then_inc(fs_t, 1)
            e.wait_ge(act_lo, 16 + FFC + 8)
            ph = PH["glu"]
            with e.Fori(0, ph.bodies) as i:
                for j in range(4):
                    free(ph, i, j)
                    tile(ph, i, j, 8, from_act(0), j, True, True, None, DEAD)
            ffn(1)
            mean_squares(NORMS["final"])
            for c in range(DC):
                e.wait_ge(yg_done, c + 1)
                if c >= 2:
                    e.wait_ge(y_c, c - 1)
                for t, (t0, n) in enumerate(((META, P), (META + P, P), (TP, NS * LS))):
                    ins = pe.transpose(bank[c % 2][0:n, t * P:(t + 1) * P], yg[:, c % 2, t0:t0 + n], ident[:])
                ins.then_inc(y_t, 1)


_INS = ["x_prompt", "x_sample", "state_a_conv", "state_a_h", "state_b_S", "state_c_re", "state_c_im", "state_ffn_conv",
        "meta_tokens", "g_mix", "w_in_e", "conv_a_w", "conv_a_b", "w_ra", "b_ra", "w_ia", "b_ia", "lam_a", "lb_logits",
        "gn_b", "w_out_e", "w_in_c", "lam_re", "lam_im", "log_dt", "bmat_re", "bmat_im", "cmat_re", "cmat_im", "d_skip",
        "w_glu_v", "w_glu_g", "g_ffn", "w_up", "w_gate", "conv_f_w", "conv_f_b", "w_down", "g_final"]
_OUTS = [("y_prompt", (1, SEQ, D)), ("y_sample", (NS, LS, D))] + [
    (f"{w}_{n}", shape(b)) for w, b in (("p", 1), ("s", NS)) for n, shape in (
        ("a_conv", lambda b: (1, b, 3, DA)), ("a_h", lambda b: (1, b, DA)), ("b_S", lambda b: (1, b, HEADS, P, P)),
        ("c_re", lambda b: (1, b, G5, P5)), ("c_im", lambda b: (1, b, G5, P5)), ("f_conv", lambda b: (2, b, 2, DFF)))]


def kernel(**inputs):
    import concourse.bacc as bacc
    from concourse.bass_utils import run_bass_kernel_spmd

    nc = bacc.Bacc("TRN2", target_bir_lowering=False, num_devices=1)
    rows = np.arange(P)
    odd = (rows // C5 % 2).astype(np.float32)
    arrays = {"c_ident": np.eye(P, dtype=np.float32),
              "c_masks": np.stack([1 - odd, odd, odd - 1, -odd], axis=1).astype(np.float32)}
    for name in _INS:
        arrays[name] = np.ascontiguousarray(inputs[name])
    a = {n: nc.dram_tensor(f"in_{n}", x.shape, mybir.dt.from_np(x.dtype), kind="ExternalInput").ap() for n, x in arrays.items()}
    o = {n: nc.dram_tensor(f"out_{n}", shape, F32, kind="ExternalOutput").ap() for n, shape in _OUTS}
    build(nc, a, o)
    r = run_bass_kernel_spmd(nc, [{f"in_{n}": x for n, x in arrays.items()}], core_ids=[0])
    return tuple(r.results[0][f"out_{n}"] for n, _ in _OUTS)
```
